# Optimizing a Trainium2 kernel written in Bass

```python
import math
import jax, jax.numpy as jnp
from jax import lax
import numpy as np

D_MODEL = 1024
BATCH = 1
SEQ = 1024
DEPTH = 2

GRID_W = 64
Q_BLOCK = 128
HEAD_DIM = 64
N_HEADS_A = 8
N_KV_A = 2
N_HEADS_B = 4
MLA_Q_RANK = 192
MLA_KV_RANK = 128
MLA_NOPE = 64
MLA_ROPE = 32
MLA_V = 64
N_HEADS_C = 4
DIFF_QK = 32
DIFF_V = 64
D_FF = 2816
CONV_W = 3
ROPE_BASE = 10000.0
EPS = 1e-6
A_WIDTH = N_HEADS_A * HEAD_DIM + 2 * N_KV_A * HEAD_DIM
B_WIDTH = MLA_Q_RANK + MLA_KV_RANK + MLA_ROPE
C_WIDTH = 2 * N_HEADS_C * 2 * DIFF_QK + N_HEADS_C * DIFF_V
IN_WIDTH = A_WIDTH + B_WIDTH + C_WIDTH
MIX_WIDTH = N_HEADS_A * HEAD_DIM + N_HEADS_B * MLA_V + N_HEADS_C * DIFF_V

kernel_name = 'hybrid_parallel_heads_encoder'

def rmsnorm(x, g):
    xf = x.astype(jnp.float32)
    y = xf * lax.rsqrt(jnp.mean(xf * xf, axis=-1, keepdims=True) + EPS)
    return (y * g.astype(jnp.float32)).astype(x.dtype)

def softmax_f32(logits, scale, dtype):
    return jax.nn.softmax(logits.astype(jnp.float32) * scale, axis=-1).astype(dtype)

def axial_rope_tables(rows, cols, dim):
    nf = dim // 4
    inv = ROPE_BASE ** (-jnp.arange(nf, dtype=jnp.float32) / nf)
    ar = rows.astype(jnp.float32)[:, None] * inv
    ac = cols.astype(jnp.float32)[:, None] * inv
    return (jnp.cos(ar), jnp.sin(ar), jnp.cos(ac), jnp.sin(ac))

def _rotate(v, c, s):
    h = v.shape[-1] // 2
    v1, v2 = v[..., :h], v[..., h:]
    return jnp.concatenate([v1 * c - v2 * s, v2 * c + v1 * s], axis=-1)

def apply_axial_rope(x, tabs):
    S = x.shape[1]
    shp = (S,) + (1,) * (x.ndim - 3) + (-1,)
    cr, sr, cc, sc = [t.reshape(shp) for t in tabs]
    xf = x.astype(jnp.float32)
    half = x.shape[-1] // 2
    out = jnp.concatenate([_rotate(xf[..., :half], cr, sr), _rotate(xf[..., half:], cc, sc)], axis=-1)
    return out.astype(x.dtype)

def to_blocks(x):
    B, S = x.shape[:2]
    return jnp.moveaxis(x.reshape((B, S // Q_BLOCK, Q_BLOCK) + x.shape[2:]), 1, 0)

def from_blocks(o):
    nb, B, blk = o.shape[:3]
    return jnp.moveaxis(o, 0, 1).reshape((B, nb * blk) + o.shape[3:])

def gqa_axial_mixer(qa, ka, va, q_gain, k_gain, tabs):
    B, S, _ = qa.shape
    G = N_HEADS_A // N_KV_A
    q = apply_axial_rope(rmsnorm(qa.reshape(B, S, N_HEADS_A, HEAD_DIM), q_gain), tabs)
    k = apply_axial_rope(rmsnorm(ka.reshape(B, S, N_KV_A, HEAD_DIM), k_gain), tabs)
    v = va.reshape(B, S, N_KV_A, HEAD_DIM)
    scale = HEAD_DIM ** -0.5

    def block(qb):
        qg = qb.reshape(qb.shape[0], Q_BLOCK, N_KV_A, G, HEAD_DIM)
        logits = jnp.einsum('bqkgd,bskd->bkgqs', qg, k)
        p = softmax_f32(logits, scale, v.dtype)
        o = jnp.einsum('bkgqs,bskd->bqkgd', p, v)
        return o.reshape(qb.shape[0], Q_BLOCK, N_HEADS_A * HEAD_DIM)

    return from_blocks(lax.map(block, to_blocks(q)))

def mla_mixer(cq, ckv, kr, q_gain, w_uq, kv_gain, w_ukv, tabs):
    B, S, _ = cq.shape
    q = (rmsnorm(cq, q_gain) @ w_uq).reshape(B, S, N_HEADS_B, MLA_NOPE + MLA_ROPE)
    qn = q[..., :MLA_NOPE]
    qr = apply_axial_rope(q[..., MLA_NOPE:], tabs)
    kv = (rmsnorm(ckv, kv_gain) @ w_ukv).reshape(B, S, N_HEADS_B, MLA_NOPE + MLA_V)
    kn, v = kv[..., :MLA_NOPE], kv[..., MLA_NOPE:]
    kr = apply_axial_rope(kr, tabs)
    scale = (MLA_NOPE + MLA_ROPE) ** -0.5

    def block(args):
        qnb, qrb = args
        logits = jnp.einsum('bqhd,bshd->bhqs', qnb, kn) + jnp.einsum('bqhr,bsr->bhqs', qrb, kr)
        p = softmax_f32(logits, scale, v.dtype)
        return jnp.einsum('bhqs,bshe->bqhe', p, v)

    o = from_blocks(lax.map(block, (to_blocks(qn), to_blocks(qr))))
    return o.reshape(B, S, N_HEADS_B * MLA_V)

def diff_alibi_mixer(qc, kc, vc, lq1, lk1, lq2, lk2, subln, lam_init, pos):
    B, S, _ = qc.shape
    q = qc.reshape(B, S, N_HEADS_C, 2, DIFF_QK)
    k = kc.reshape(B, S, N_HEADS_C, 2, DIFF_QK)
    v = vc.reshape(B, S, N_HEADS_C, DIFF_V)
    f32 = jnp.float32
    lam = (jnp.exp(jnp.sum(lq1.astype(f32) * lk1.astype(f32)))
           - jnp.exp(jnp.sum(lq2.astype(f32) * lk2.astype(f32))) + lam_init)
    slopes = 2.0 ** (-8.0 * jnp.arange(1, N_HEADS_C + 1, dtype=f32) / N_HEADS_C)
    scale = DIFF_QK ** -0.5

    def block(args):
        qb, qp = args
        logits = jnp.einsum('bqhid,bshid->bhiqs', qb, k).astype(f32) * scale
        bias = -slopes[:, None, None, None] * jnp.abs(qp[:, None] - pos[None, :])[None, None]
        p = jax.nn.softmax(logits + bias, axis=-1)
        a = (p[:, :, 0] - lam * p[:, :, 1]).astype(v.dtype)
        return jnp.einsum('bhqs,bshe->bqhe', a, v)

    o = from_blocks(lax.map(block, (to_blocks(q), pos.reshape(S // Q_BLOCK, Q_BLOCK))))
    o = rmsnorm(o, subln) * (1.0 - lam_init)
    return o.reshape(B, S, N_HEADS_C * DIFF_V)

def conv_gated_mlp(h, w_up, conv_w, conv_b, w_down):
    u = h @ w_up
    up = jnp.pad(u, ((0, 0), (1, 1), (0, 0)))
    u = up[:, :-2] * conv_w[0] + up[:, 1:-1] * conv_w[1] + up[:, 2:] * conv_w[2] + conv_b
    g, val = u[..., :D_FF], u[..., D_FF:]
    return (jax.nn.silu(g) * val) @ w_down

def setup_inputs(seed: int = 0) -> dict:
    key = jax.random.key(seed)
    ks = jax.random.split(key, 21)

    def nrm(k, shape, scale):
        return scale * jax.random.normal(k, shape, jnp.float32)

    def gain(k, shape):
        return 1.0 + 0.02 * jax.random.normal(k, shape, jnp.float32)

    L = DEPTH
    return dict(
        x=jax.random.normal(ks[0], (BATCH, SEQ, D_MODEL), jnp.float32),
        norm_attn=gain(ks[1], (L, D_MODEL)),
        w_in=nrm(ks[2], (L, D_MODEL, IN_WIDTH), D_MODEL ** -0.5),
        q_norm_a=gain(ks[3], (L, HEAD_DIM)),
        k_norm_a=gain(ks[4], (L, HEAD_DIM)),
        q_a_norm_b=gain(ks[5], (L, MLA_Q_RANK)),
        w_uq_b=nrm(ks[6], (L, MLA_Q_RANK, N_HEADS_B * (MLA_NOPE + MLA_ROPE)), MLA_Q_RANK ** -0.5),
        kv_a_norm_b=gain(ks[7], (L, MLA_KV_RANK)),
        w_ukv_b=nrm(ks[8], (L, MLA_KV_RANK, N_HEADS_B * (MLA_NOPE + MLA_V)), MLA_KV_RANK ** -0.5),
        lambda_q1_c=nrm(ks[9], (L, DIFF_QK), 0.1),
        lambda_k1_c=nrm(ks[10], (L, DIFF_QK), 0.1),
        lambda_q2_c=nrm(ks[11], (L, DIFF_QK), 0.1),
        lambda_k2_c=nrm(ks[12], (L, DIFF_QK), 0.1),
        subln_c=gain(ks[13], (L, DIFF_V)),
        w_out=nrm(ks[14], (L, MIX_WIDTH, D_MODEL), MIX_WIDTH ** -0.5),
        norm_ffn=gain(ks[15], (L, D_MODEL)),
        w_up=nrm(ks[16], (L, D_MODEL, 2 * D_FF), D_MODEL ** -0.5),
        conv_w=nrm(ks[17], (L, CONV_W, 2 * D_FF), CONV_W ** -0.5),
        conv_b=nrm(ks[18], (L, 2 * D_FF), 0.01),
        w_down=nrm(ks[19], (L, D_FF, D_MODEL), D_FF ** -0.5),
        final_norm=gain(ks[20], (D_MODEL,)),
    )

def reference(x, norm_attn, w_in, q_norm_a, k_norm_a, q_a_norm_b, w_uq_b, kv_a_norm_b, w_ukv_b,
              lambda_q1_c, lambda_k1_c, lambda_q2_c, lambda_k2_c, subln_c, w_out,
              norm_ffn, w_up, conv_w, conv_b, w_down, final_norm):
    B, S, _ = x.shape
    ROWS = S // GRID_W
    rows = jnp.repeat(jnp.arange(ROWS, dtype=jnp.int32), GRID_W)
    cols = jnp.tile(jnp.arange(GRID_W, dtype=jnp.int32), ROWS)
    tabs_a = axial_rope_tables(rows, cols, HEAD_DIM)
    tabs_b = axial_rope_tables(rows, cols, MLA_ROPE)
    pos = jnp.arange(S, dtype=jnp.float32)
    sizes = [N_HEADS_A * HEAD_DIM, N_KV_A * HEAD_DIM, N_KV_A * HEAD_DIM,
             MLA_Q_RANK, MLA_KV_RANK, MLA_ROPE,
             N_HEADS_C * 2 * DIFF_QK, N_HEADS_C * 2 * DIFF_QK, N_HEADS_C * DIFF_V]
    splits = [int(c) for c in np.cumsum(sizes)[:-1]]

    for l in range(DEPTH):
        lam_init = 0.8 - 0.6 * math.exp(-0.3 * l)
        h = rmsnorm(x, norm_attn[l])
        z = h @ w_in[l]
        qa, ka, va, cq, ckv, kr, qc, kc, vc = jnp.split(z, splits, axis=-1)
        o_a = gqa_axial_mixer(qa, ka, va, q_norm_a[l], k_norm_a[l], tabs_a)
        o_b = mla_mixer(cq, ckv, kr, q_a_norm_b[l], w_uq_b[l], kv_a_norm_b[l], w_ukv_b[l], tabs_b)
        o_c = diff_alibi_mixer(qc, kc, vc, lambda_q1_c[l], lambda_k1_c[l], lambda_q2_c[l],
                               lambda_k2_c[l], subln_c[l], lam_init, pos)
        x = x + jnp.concatenate([o_a, o_b, o_c], axis=-1) @ w_out[l]
        h = rmsnorm(x, norm_ffn[l])
        x = x + conv_gated_mlp(h, w_up[l], conv_w[l], conv_b[l], w_down[l])

    return rmsnorm(x, final_norm)


_drawn_inputs = setup_inputs


def setup_inputs(seed=0):
    import zlib

    import numpy as np

    out = dict(_drawn_inputs(seed))
    spreads = {}
    factors = {'norm_attn': 2.745,
     'q_norm_a': 8.0,
     'k_norm_a': 8.0,
     'q_a_norm_b': 8.0,
     'kv_a_norm_b': 8.0,
     'lambda_q1_c': 4.842,
     'lambda_k1_c': 8.0,
     'subln_c': 5.061,
     'norm_ffn': 2.681,
     'conv_b': 5.476,
     'final_norm': 2.952}
    for name, (base, spread) in spreads.items():
        noise = np.random.default_rng([zlib.crc32(name.encode()), seed]).standard_normal(out[name].shape)
        drawn = base * np.exp(spread * noise) if base else spread * noise
        out[name] = __import__('jax').numpy.asarray(drawn.astype(out[name].dtype))
    for name, factor in factors.items():
        out[name] = (out[name] * factor).astype(out[name].dtype)
    return out
```

```python
from contextlib import ExitStack

import numpy as np

import concourse.bass as bass
from concourse import mybir

F32 = mybir.dt.float32
F32R = mybir.dt.float32r
F16 = mybir.dt.float16
ALU = mybir.AluOpType
ACT = mybir.ActivationFunctionType
AX = mybir.AxisListType

P = 128
L, T, D = 2, 1024, 1024
KT = D // P
TT = T // P
HALF = 512
HD = 64
NA, NKV, NB, NC = 8, 2, 4, 4
QR, KVR, NOPE, ROPE = 192, 128, 64, 32
CQK = 32
FF = 2816
FT = FF // P
GROUPS = FT // 2
EPS = 1e-6
GRID_W = 64

A_Q, A_K, A_V = 0, 512, 640
B_CQ, B_CKV, B_KR = 768, 960, 1088
C_Q, C_K, C_V = 1120, 1376, 1632
IN_W = 1888

TILES = [("cq0", B_CQ), ("cq1", B_CQ + P), ("ckv", B_CKV), ("kr", B_KR)]
TILES += [("aq", A_Q + P * i) for i in range(4)] + [("ak", A_K)]
TILES += [("cq_", C_Q), ("cq_", C_Q + P), ("ck_", C_K), ("ck_", C_K + P)]
TILES += [("v", A_V), ("v", C_V), ("v", C_V + P)]
NT = len(TILES)
ITEMS = [0, 1, 2, 3, "uq", "ukv"] + list(range(4, NT))
NI = len(ITEMS)
JOBS = {0: [("sx", 0)], 2: [("scq", 0)], 3: [("sckv", 0)], 4: [("uq", h) for h in range(4)],
        5: [("sa", 4), ("ukv", 0), ("ukv", 1), ("tr", 0), ("ukv", 2), ("tr", 1), ("ukv", 3), ("tr", 2), ("tr", 3)],
        6: [("sa", 5)], 7: [("sa", 6)], 8: [("sa", 7)], 9: [("sa", 8)],
        14: [("tv", 13)], 15: [("tv", 14), ("tv", 15)]}
JOB_LIST = [j for t in range(NT) for j in JOBS.get(t, [])]
NJ = len(JOB_LIST)
SQUARED = [0, 1, 2, 4, 5, 6, 7, 8]

V_NEXT, V_FFN, V_QG, V_KG, V_CQG, V_CKVG, V_SUB, V_LAM = 0, 8, 16, 17, 18, 20, 21, 22
V_CONV = V_LAM + 4 * CQK
V_LI = V_CONV + 4 * 2 * FT
VW = V_LI + 2
C_ID, C_ONE, C_BLK, C_SC, C_EPS = 0, P, 2 * P, 3 * P, 3 * P + 4
CW = C_EPS + 1
DW = 2 * T - P

SLOPES = [2.0 ** (-8.0 * (h + 1) / NC) for h in range(NC)]
SCALE_A = HD ** -0.5
SCALE_B = (NOPE + ROPE) ** -0.5
SCALE_C = CQK ** -0.5

HEADS = [("A", h) for h in range(NA)] + [("B", h) for h in range(NB)] + [("C", h) for h in range(NC)]
NU = 2 * len(HEADS)
U_C = 2 * (NA + NB)


def items_before(u):
    return 4 * u + 4 * (u - U_C) if isinstance(u, int) and u > U_C else u * 4


NS = 4 * NU + 4 * (NU - U_C)
STEP_OF = {4: {0: 0, 1: 1, 3: 2, 5: 3}, 8: {s: s for s in range(8)}}
USES = NA + NB + 2 * NC
STEPS = {"pool layer": 64, "pool pair": 6, "dve layer": 430, "dve pair": 24, "dve group": 6}
PT_CREDIT, EXP_CREDIT, AV_CREDIT, O_CREDIT = 2, 2, 4, 1
LAG = 2
NPT = 4


def build(nc, x_in, first_gain, w_in, w_uq, w_ukv, w_out, w_up, w_down, vecs, consts, dist, rope_a, rope_b, out):
    def dram(name, shape):
        return nc.dram_tensor(name, shape, F32).ap()

    qa_d, ka_d = dram("qa_d", (NA * HD, T)), dram("ka_d", (NKV * HD, T))
    qb_d, kb_d = dram("qb_d", (NB * 96, T)), dram("kb_d", (NB * 96, T))
    qc_d, kc_d = dram("qc_d", (NC * 2 * CQK, T)), dram("kc_d", (NC * 2 * CQK, T))
    v_d = dram("v_d", (T, (NKV + NC + NB) * HD))
    x_d = dram("x_d", (KT, P, T))

    ctx = ExitStack()
    with ctx:
        def sb(stack, name, shape, dt=F32):
            return stack.enter_context(nc.sbuf_tensor(name, shape, dt))

        xgh, xgl = sb(ctx, "xgh", [P, KT, T], F32R), sb(ctx, "xgl", [P, KT, T], F32R)
        vec, cst = sb(ctx, "vec", [P, VW]), sb(ctx, "cst", [P, CW])
        gain0 = sb(ctx, "gain0", [P, KT])
        small = sb(ctx, "small", [P, 8])
        ident, ones, blk = cst[:, C_ID:C_ID + P], cst[:, C_ONE:C_ONE + P], cst[:, C_BLK:C_BLK + P]
        eps = cst[:, C_EPS:C_EPS + 1]

        ph13 = ExitStack()
        xT, rstd = sb(ph13, "xT", [P, KT, T]), sb(ph13, "rstd", [P, T])

        ph1 = ExitStack()
        wraw = sb(ph1, "wraw", [P, 2, KT * P])
        wh, wl = sb(ph1, "wh", [P, 2, KT * P], F32R), sb(ph1, "wl", [P, 2, KT * P], F32R)
        ra, rb_ = sb(ph1, "ra", [P, 2, T]), sb(ph1, "rb_", [P, 2, T])
        z, sq, r = sb(ph1, "z", [P, 2, T]), sb(ph1, "sq", [P, T]), sb(ph1, "r", [P, T])
        e = sb(ph1, "e", [P, 2, T])
        vt = sb(ph1, "vt", [P, TT, P])
        ch, cl = sb(ph1, "ch", [P, 3, T], F32R), sb(ph1, "cl", [P, 3, T], F32R)
        wqh, wql = sb(ph1, "wqh", [P, 2, 384], F32R), sb(ph1, "wql", [P, 2, 384], F32R)
        wkh, wkl = sb(ph1, "wkh", [P, 512], F32R), sb(ph1, "wkl", [P, 512], F32R)
        ph1.close()

        ph3 = ExitStack()
        upraw = sb(ph3, "upraw", [P, 2 * KT * P])
        uph, upl = sb(ph3, "uph", [P, 2, 2 * KT * P], F32R), sb(ph3, "upl", [P, 2, 2 * KT * P], F32R)
        draw = sb(ph3, "draw", [P, 2, D])
        dnh, dnl = sb(ph3, "dnh", [P, 2, D], F32R), sb(ph3, "dnl", [P, 2, D], F32R)
        ah, al = sb(ph3, "ah", [P, 2, T], F32R), sb(ph3, "al", [P, 2, T], F32R)
        u, cv = sb(ph3, "u", [P, 2, T + 2]), sb(ph3, "cv", [P, 2, T])
        sq3 = sb(ph3, "sq3", [P, T])
        ph3.close()
        ph13.close()

        ph2 = ExitStack()
        oc = sb(ph2, "oc", [P, 2, T])
        prob, prob1 = sb(ph2, "prob", [P, 2, 4, T]), sb(ph2, "prob1", [P, T])
        pth, ptl = sb(ph2, "pth", [P, NPT, HALF], F32R), sb(ph2, "ptl", [P, NPT, HALF], F32R)
        stack = [[sb(ph2, f"stack{p}{s}", [P, T], F32R) for s in range(4)] for p in range(2)]
        raw = sb(ph2, "raw", [P, 2, T])
        vraw = sb(ph2, "vraw", [P, TT, HD])
        vst = [sb(ph2, f"vst{p}", [P, TT, P], F32R) for p in range(2)]
        dtab = sb(ph2, "dtab", [P, DW], F16)
        diag, osum, obot = sb(ph2, "diag", [P, 4, P]), sb(ph2, "osum", [HD, HALF]), sb(ph2, "obot", [HD, HALF])
        ohi = sb(ph2, "ohi", [HD, HALF], F32R)
        mx, nmx = sb(ph2, "mx", [P, 2, 8]), sb(ph2, "nmx", [P, 2, 8])
        rsum, rinv = sb(ph2, "rsum", [P, 2, 8]), sb(ph2, "rinv", [P, 2, 8])
        ph2.close()

        ps = ctx.enter_context(nc.psum_tensor("ps", [P, 8, HALF], F32))

        def sem(name):
            return ctx.enter_context(nc.semaphore(name))

        fence = sem("fence")
        settled = {n: sem("settled_" + n) for n in ("PE", "DVE", "Activation", "Pool", "SP")}
        x_loaded, const_loaded, vec_loaded = sem("x_loaded"), sem("const_loaded"), sem("vec_loaded")
        dve_step, pool_step = sem("dve_step"), sem("pool_step")
        xt_done, xt_copied = sem("xt_done"), sem("xt_copied")
        x_final, x_squared, sq_added, xg_hi, xg_lo = (sem(n) for n in ("x_final", "x_squared", "sq_added", "xg_hi", "xg_lo"))
        wraw_full = [sem("wraw_full0"), sem("wraw_full1")]
        w_hi, w_lo, proj_done, z_ready = sem("w_hi"), sem("w_lo"), sem("proj_done"), sem("z_ready")
        sq_ready, sq_free, job_ready, job_free = sem("sq_ready"), sem("sq_free"), sem("job_ready"), sem("job_free")
        r_free, latent_ready, out_ready = sem("r_free"), sem("latent_ready"), sem("out_ready")
        roped, z_stored, e_stored = sem("roped"), [sem("z_stored0"), sem("z_stored1")], [sem("e_stored0"), sem("e_stored1")]
        vt_stored, x_stored, rope_loaded = sem("vt_stored"), sem("x_stored"), sem("rope_loaded")
        raw_full, raw_free = [sem("rawq_full"), sem("rawk_full")], [sem("rawq_free"), sem("rawk_free")]
        vraw_full, vraw_free = sem("vraw_full"), sem("vraw_free")
        dtab_loaded = sem("dtab_loaded")
        scores_done, max_done, exp_done, mixed = sem("scores_done"), sem("max_done"), sem("exp_done"), sem("mixed")
        trans_done, pt_hi, pt_lo, av_done = sem("trans_done"), sem("pt_hi"), sem("pt_lo"), sem("av_done")
        diag_done, norm_done, bot_copied, o_read, o_ready, mix_hi, mix_lo = (
            sem(n) for n in ("diag_done", "norm_done", "bot_copied", "o_read", "o_ready", "mix_hi", "mix_lo"))
        lam_exp = sem("lam_exp")
        up_full, up_hi, up_lo, dn_full, dn_hi, dn_lo = (sem(n) for n in ("up_full", "up_hi", "up_lo", "dn_full", "dn_hi", "dn_lo"))
        x_back = [sem(f"x_back{t}") for t in range(KT)]
        c_squared, c_stat, c_root, c_root_free, c_normed, c_hi, c_lo = (
            sem(n) for n in ("c_squared", "c_stat", "c_root", "c_root_free", "c_normed", "c_hi", "c_lo"))
        op_done, stat_done, root_done, rstd_done = sem("op_done"), sem("stat_done"), sem("root_done"), sem("rstd_done")
        up_done, u_ready, tap_mid, conv_done, silu_done, prod_done, a_hi, a_lo = (
            sem(n) for n in ("up_done", "u_ready", "tap_mid", "conv_done", "silu_done", "prod_done", "a_hi", "a_lo"))
        down_done, y_done = sem("down_done"), sem("y_done")
        fin_ready, fin_trans, fin_copied, out_stored = sem("fin_ready"), sem("fin_trans"), sem("fin_copied"), [sem("out_stored0"), sem("out_stored1")]

        
        def settle(eng):
            eng.sem_inc(settled[eng.engine.name], 1)

        def meet(eng, l, n):
            settle(eng)
            eng.drain().then_inc(fence, 1)
            eng.wait_ge(fence, l * 15 + 5 * n + 5)

        class Steps:

            def __init__(self, eng, s):
                self.eng, self.s, self.base, self.n = eng, s, 0, 0

            def __call__(self, ins):
                self.n += 1
                ins.then_inc(self.s, 1)
                self.eng.wait_ge(self.s, self.base + self.n)

            def enter(self, i, loop, first=0):
                was = (self.base, self.n)
                self.base, self.n = (i - first) * STEPS[loop] + (self.base + self.n), 0
                return was

            def leave(self, was, loop, passes):
                assert self.n == STEPS[loop], f"STEPS {loop} = {self.n}"
                self.base, self.n = was[0], was[1] + STEPS[loop] * passes

        def raw_dmas(n):
            return sum(2 if ITEMS[m] == "uq" else 1 for m in range(n % 2, n + 1, 2))

        RAWS = [raw_dmas(NI - 2 + (NI + p) % 2) for p in range(2)]
        Z_OUT = [t for t in range(NT) if TILES[t][0] in ("kr", "aq", "ak", "cq_", "ck_")]

        def z_dmas(t):
            return NB if TILES[t][0] == "kr" else 1

        def z_stores(t):
            return sum(z_dmas(m) for m in Z_OUT if m <= t and m % 2 == t % 2)

        ZS = [z_stores(14), z_stores(15)]

        def job_no(kind, a):
            return JOB_LIST.index((kind, a))

        READY = [x for x in JOB_LIST if x[0] not in ("scq", "sckv", "sa")]
        NR = len(READY)

        def ready_no(kind, a):
            return READY.index((kind, a))

        def item_no(t):
            return ITEMS.index(t)

        stage = [z[:, 0, :], z[:, 1, :], e[:, 0, :], e[:, 1, :], ra[:, 0, :], ra[:, 1, :], rb_[:, 0, :], rb_[:, 1, :]]

        def two(ap):
            return ap.rearrange("p (b n) -> p b n", b=2)

        def staged(group, n):
            return n * {"A": 2, "B": 1, "C": 4}[group] + {"A": 2, "B": 2 * NA + 1, "C": 2 * NA + NB + 4}[group]

        STAGED = 2 * NA + NB + 4 * 2 * NC
        USE0 = {"A": 0, "B": NA, "C": NA + NB}
        HEAD0 = {"A": 0, "B": NA, "C": NA + NB}

        LAST_PAIRS = [("A", 3, "B"), ("B", 0, "B"), ("B", 1, "C"), ("C", 0, "C"), ("C", 1, None)]

        def unit(group, pair, k):
            first = {"A": 0, "B": 2 * NA, "C": U_C}[group]
            u_ = pair * 4 + (first + k)
            return dict(group=group, par=k // 2, half=k % 2, u=u_, h=pair * 2 + k // 2, pair=pair,
                        tile=pair + HEAD0[group] // 2, items=8 if group == "C" else 4, item0=items_before(u_))

        def run_pairs(eng, unit_fn, step=None):
            def pair_units(group, pair, nxt):
                for k in range(4):
                    if k < 3:
                        n = unit(group, pair, k + 1)
                    elif nxt is None:
                        n = None
                    else:
                        n = unit(nxt, pair + 1 if nxt == group else 0, 0)
                    unit_fn(unit(group, pair, k), n)

            with eng.Fori(0, 3) as j:
                was = step.enter(j, "dve pair") if step else None
                pair_units("A", j, "A")
            if step:
                step.leave(was, "dve pair", 3)
            for group, pair, nxt in LAST_PAIRS:
                pair_units(group, pair, nxt)

        def mix_at(t_, x):
            p0, c0 = HD * x["par"], x["half"] * HALF
            return t_[p0:p0 + HD, bass.ds(x["tile"], 1), c0:c0 + HALF].rearrange("p a n -> p (a n)")

        block = ctx.enter_context(nc.Block())

        @block.sync
        def _(sp):
            sp.dma_start(cst[:, :], consts).then_inc(const_loaded, 16)
            sp.dma_start(gain0[:, :], first_gain).then_inc(const_loaded, 16)
            for m in range(TT):
                sp.dma_start(stage[m], x_in[m * P:(m + 1) * P, :]).then_inc(x_loaded, 16)
            meet(sp, 0, 0)

            with sp.Fori(0, L) as l:
                def raw_load(n):
                    if n >= 2:
                        sp.wait_ge(w_lo, l * NI + n - 1)
                        settle(sp)
                    it = ITEMS[n]
                    if it == "uq":
                        sp.dma_start(wraw[:, n % 2, 0:384], w_uq[bass.ds(l, 1), 0:P, :].rearrange("a p n -> p (a n)")).then_inc(wraw_full[n % 2], 16)
                        sp.dma_start(wraw[0:QR - P, n % 2, 384:768], w_uq[bass.ds(l, 1), P:QR, :].rearrange("a p n -> p (a n)")).then_inc(wraw_full[n % 2], 16)
                    elif it == "ukv":
                        sp.dma_start(wraw[:, n % 2, 0:512], w_ukv[bass.ds(l, 1), :, :].rearrange("a p n -> p (a n)")).then_inc(wraw_full[n % 2], 16)
                    else:
                        c = TILES[it][1]
                        sp.dma_start(wraw[:, n % 2, :].rearrange("p (k n) -> p k n", k=KT),
                                     w_in[bass.ds(l, 1), :, c:c + P].rearrange("a (k p) n -> p (a k) n", p=P)).then_inc(wraw_full[n % 2], 16)

                raw_load(0)
                raw_load(1)
                sp.dma_start(vec[:, :], vecs[bass.ds(l, 1), :, :].rearrange("a p n -> p (a n)")).then_inc(vec_loaded, 16)
                for i in range(2):
                    sp.dma_start(ra[:, i, :], rope_a[i]).then_inc(rope_loaded, 16)
                    for p0 in (0, 64):
                        sp.dma_start(rb_[p0:p0 + ROPE, i, :], rope_b[i]).then_inc(rope_loaded, 16)
                sp.dma_start(x_d.rearrange("k p t -> p k t"), xT[:, :, :]).then_inc(x_stored, 16)

                def store_z(t):
                    if t <= 8:
                        sp.wait_ge(out_ready, l * 6 + t - 2)
                    else:
                        sp.wait_ge(z_ready, l * NT + t + 1)
                    kind = TILES[t][0]
                    if kind == "kr":
                        for h in range(NB):
                            sp.dma_start(kb_d[h * 96 + NOPE:(h + 1) * 96, :], z[0:ROPE, t % 2, :]).then_inc(z_stored[t % 2], 16)
                        return
                    dst = {"aq": qa_d, "ak": ka_d, "cq_": qc_d, "ck_": kc_d}[kind]
                    n = [m for m in range(NT) if TILES[m][0] == kind].index(t)
                    sp.dma_start(dst[n * P:(n + 1) * P, :], z[:, t % 2, :]).then_inc(z_stored[t % 2], 16)

                def store_job(kind, h):
                    if kind == "uq":
                        sp.wait_ge(roped, l * NB + h + 1)
                        sp.dma_start(qb_d[h * 96:(h + 1) * 96, :], e[0:96, h % 2, :]).then_inc(e_stored[h % 2], 16)
                        return
                    sp.wait_ge(job_free, l * NJ + job_no(kind, h) + 1)
                    v_rows = v_d.rearrange("(m p) c -> p m c", p=P)
                    if kind == "ukv":
                        sp.dma_start(kb_d[h * 96:h * 96 + NOPE, :], e[0:NOPE, h % 2, :]).then_inc(e_stored[h % 2], 16)
                    elif kind == "tr":
                        sp.dma_start(v_rows[:, :, (6 + h) * HD:(7 + h) * HD], vt[:, :, 0:HD]).then_inc(vt_stored, 16)
                    else:
                        sp.dma_start(v_rows[:, :, (h - 13) * P:(h - 12) * P], vt[:, :, :]).then_inc(vt_stored, 16)

                n = 2
                for t in range(NT):
                    while n < NI and n <= item_no(t) + 2:
                        raw_load(n)
                        n += 1
                    if t == 4:
                        store_z(3)
                    if t == 5:
                        for h in range(NB):
                            store_job("uq", h)
                    if t == 6:
                        for kind, h in JOBS[5][1:]:
                            store_job(kind, h)
                    if 6 <= t <= 10:
                        store_z(t - 2)
                    if 11 <= t <= 14:
                        store_z(t - 2)
                for kind, h in JOBS[14] + JOBS[15]:
                    store_job(kind, h)
                for p in range(2):
                    sp.wait_ge(z_stored[p], l * (16 * ZS[p]) + 16 * ZS[p])
                    sp.wait_ge(e_stored[p], l * 64 + 64)
                settle(sp)
                sp.wait_ge(vt_stored, l * (7 * 16) + 7 * 16)
                settle(sp)
                sp.wait_ge(x_stored, l * 16 + 16)
                meet(sp, l, 1)

                sp.dma_start(dtab[:, :], dist).then_inc(dtab_loaded, 16)

                def load_head(group, h, v):
                    src_q, src_k, rows, copies = {"A": (qa_d, ka_d, HD, 2), "B": (qb_d, kb_d, 96, 1), "C": (qc_d, kc_d, CQK, 4)}[group]
                    maps = 2 if group == "C" else 1
                    for i in range(maps):
                        n_ = h * maps + i
                        for s, (src, row) in enumerate(((src_q, n_ * rows), (src_k, (v if group == "A" else n_) * rows))):
                            sp.wait_ge(raw_free[s], l * USES + USE0[group] + n_ + 1)
                            for c in range(copies):
                                sp.dma_start(raw[c * (P // copies):c * (P // copies) + rows, s, :], src[bass.ds(row, rows), :]).then_inc(raw_full[s], 16)
                    sp.wait_ge(vraw_free, l * (NA + NB + NC) + HEAD0[group] + h + 1)
                    settle(sp)
                    col = {"A": v, "B": h + 6, "C": h + 2}[group] * HD
                    sp.dma_start(vraw[:, :, :], v_d.rearrange("(m p) c -> p m c", p=P)[:, :, bass.ds(col, HD)]).then_inc(vraw_full, 16)

                with sp.Fori(0, NKV) as g:
                    with sp.Fori(0, NA // NKV) as hh:
                        load_head("A", g * (NA // NKV) + hh, g)
                with sp.Fori(0, NB) as h:
                    load_head("B", h, h)
                with sp.Fori(0, NC) as h:
                    load_head("C", h, h)
                meet(sp, l, 2)

                def load_out(t):
                    if t:
                        sp.wait_ge(up_lo, l * (KT + FT) + t)
                    sp.dma_start(upraw[:, 0:KT * P].rearrange("p (k n) -> p k n", k=KT),
                                 w_out[bass.ds(l, 1), :, t * P:(t + 1) * P].rearrange("a (k p) n -> p (a k) n", p=P)).then_inc(up_full, 16)

                def load_up(f):
                    sp.wait_ge(up_lo, l * (KT + FT) + KT + f)
                    v3 = upraw[:, :].rearrange("p (k c n) -> p k c n", k=KT, c=2)
                    for c in range(2):
                        sp.dma_start(v3[:, :, c, :], w_up[bass.ds(l, 1), :, bass.ds(f * P + c * FF, P)].rearrange("a (k p) n -> p (a k) n", p=P)).then_inc(up_full, 16)

                def load_down(g):
                    if not (isinstance(g, int) and g == 0):
                        sp.wait_ge(dn_lo, l * GROUPS + g)
                    sp.dma_start(draw[:, :, :], w_down[bass.ds(l, 1), bass.ds(g * (2 * P), 2 * P), :].rearrange("a (c p) n -> p (a c) n", p=P)).then_inc(dn_full, 16)

                load_out(0)
                for t in range(2, KT):
                    sp.dma_start(xT[:, t, :], x_d[t]).then_inc(x_back[t], 16)
                load_down(0)
                for t in range(1, KT):
                    load_out(t)
                    if t == 1:
                        for c in range(2):
                            sp.wait_ge(c_normed, l * 2 + 2)
                            sp.dma_start(xT[:, c, :], x_d[c]).then_inc(x_back[c], 16)
                for f in range(3):
                    load_up(f)
                with sp.Fori(1, GROUPS - 1) as i:
                    load_up(i * 2 + 1)
                    load_up(i * 2 + 2)
                    load_down(i)
                load_up(FT - 1)
                load_down(GROUPS - 1)
                meet(sp, l, 3)
                settle(sp)

            for t in range(KT):
                sp.wait_ge(fin_copied, t + 1)
                sp.dma_start(out.rearrange("(m p) d -> p m d", p=P)[:, :, t * P:(t + 1) * P],
                             e[:, t % 2, :].rearrange("p (m d) -> p m d", m=TT)).then_inc(out_stored[t % 2], 16)
            sp.wait_ge(out_stored[0], 16 * KT // 2)
            sp.wait_ge(out_stored[1], 16 * KT // 2)

        @block.gpsimd
        def _(pool):
            step = Steps(pool, pool_step)
            for s in (raw_free[0], raw_free[1], vraw_free):
                pool.memset(small[0:1, 7:8], 0.0).then_inc(s, 1)
                pool.wait_ge(s, 1)

            def add_squares(n0, s0, sq_buf):
                for t in range(1, KT):
                    pool.wait_ge(x_squared, n0 + t + 1)
                    if t > 1:
                        pool.wait_ge(sq_added, s0 + t - 1)
                    pool.tensor_tensor(rstd[:, :], rstd[:, :], sq_buf, ALU.add).then_inc(sq_added, 1)

            add_squares(0, 0, sq[:, :])
            meet(pool, 0, 0)

            with pool.Fori(0, L) as l:
                was = step.enter(l, "pool layer")
                for n, it in enumerate(ITEMS):
                    pool.wait_ge(w_hi, l * NI + n + 1)
                    w = wraw[:, n % 2, :]
                    if it == "uq":
                        pool.tensor_tensor(wql[:, 0, :], w[:, 0:384], wqh[:, 0, :].bitcast(F32), ALU.subtract)
                        pool.tensor_tensor(wql[0:64, 1, :], w[0:64, 384:768], wqh[0:64, 1, :].bitcast(F32), ALU.subtract).then_inc(w_lo, 1)
                    elif it == "ukv":
                        pool.tensor_tensor(wkl[:, :], w[:, 0:512], wkh[:, :].bitcast(F32), ALU.subtract).then_inc(w_lo, 1)
                    else:
                        pool.tensor_tensor(wl[:, it % 2, :], w, wh[:, it % 2, :].bitcast(F32), ALU.subtract).then_inc(w_lo, 1)
                meet(pool, l, 1)

                def split(dst, src, rows=slice(0, P), lo=None):
                    settle(pool)
                    step(pool.tensor_copy(dst[rows, :], src[rows, :]))
                    for a, b in lo or ():
                        ins = pool.tensor_tensor(dst[a:b, :], src[a:b, :], dst[a:b, :].bitcast(F32), ALU.subtract)
                        step(ins) if (a, b) != lo[-1] else None
                    return ins if lo else None

                def prepare(group, h, par):
                    st = stack[par]
                    hh = h + HEAD0[group]
                    if not isinstance(hh, int) or hh >= 2:
                        pool.wait_ge(av_done, l * (8 * NU) + hh * 16 - 16 + AV_CREDIT)
                    maps = 2 if group == "C" else 1
                    for i in range(maps):
                        n_ = h * maps + i
                        pool.wait_ge(raw_full[0], (l * STAGED + staged(group, n_)) * 16)
                        q, k = raw[:, 0, :], raw[:, 1, :]
                        if group == "A":
                            split(st[0], q, lo=[(64, 128)]).then_inc(raw_free[0], 1)
                        elif group == "B":
                            settle(pool)
                            step(pool.tensor_copy(st[0][0:96, :], q[0:96, :]))
                            pool.tensor_tensor(st[1][0:96, :], q[0:96, :], st[0][0:96, :].bitcast(F32), ALU.subtract).then_inc(raw_free[0], 1)
                        else:
                            split(st[2 * i], q, lo=[(32, 64), (96, 128)]).then_inc(raw_free[0], 1)
                        pool.wait_ge(raw_free[0], l * USES + n_ + USE0[group] + 2)
                        pool.wait_ge(raw_full[1], (l * STAGED + staged(group, n_)) * 16)
                        if group == "A":
                            settle(pool)
                            step(pool.tensor_copy(st[1][:, :], k))
                            pool.tensor_tensor(st[2][:, :], k, st[1][:, :].bitcast(F32), ALU.subtract).then_inc(raw_free[1], 1)
                        elif group == "B":
                            settle(pool)
                            step(pool.tensor_copy(st[2][0:96, :], k[0:96, :]))
                            pool.tensor_tensor(st[3][0:96, :], k[0:96, :], st[2][0:96, :].bitcast(F32), ALU.subtract).then_inc(raw_free[1], 1)
                        else:
                            split(st[2 * i + 1], k, lo=[(64, 128)]).then_inc(raw_free[1], 1)
                        pool.wait_ge(raw_free[1], l * USES + n_ + USE0[group] + 2)
                    pool.wait_ge(vraw_full, (l * (NA + NB + NC) + hh + 1) * 16)
                    v = vst[par]
                    settle(pool)
                    step(pool.tensor_copy(v[:, :, 0:HD], vraw[:, :, :]))
                    ins = pool.tensor_tensor(v[:, :, HD:P], vraw[:, :, :], v[:, :, 0:HD].bitcast(F32), ALU.subtract)
                    ins.then_inc(vraw_free, 1)

                for par in range(2):
                    prepare("A", par, par)
                with pool.Fori(1, NA // 2) as j:
                    w2 = step.enter(j, "pool pair", 1)
                    for par in range(2):
                        prepare("A", j * 2 + par, par)
                step.leave(w2, "pool pair", NA // 2 - 1)
                for h in range(NB):
                    prepare("B", h, h % 2)
                for h in range(NC):
                    prepare("C", h, h % 2)
                meet(pool, l, 2)

                def lo_up(f, par):
                    pool.wait_ge(up_hi, l * (KT + FT) + KT + f + 1)
                    pool.tensor_tensor(upl[:, par, :], upraw[:, :], uph[:, par, :].bitcast(F32), ALU.subtract).then_inc(up_lo, 1)

                def lo_down(g):
                    pool.wait_ge(dn_hi, l * GROUPS + g + 1)
                    pool.tensor_tensor(dnl[:, :, :], draw[:, :, :], dnh[:, :, :].bitcast(F32), ALU.subtract).then_inc(dn_lo, 1)

                def add_square(t):
                    pool.wait_ge(x_squared, l * 16 + 8 + t + 1)
                    if t > 1:
                        pool.wait_ge(sq_added, l * 14 + 7 + t - 1)
                    pool.tensor_tensor(rstd[:, :], rstd[:, :], sq3[:, :], ALU.add).then_inc(sq_added, 1)

                for t in range(KT):
                    pool.wait_ge(up_hi, l * (KT + FT) + t + 1)
                    pool.tensor_tensor(upl[:, t % 2, 0:KT * P], upraw[:, 0:KT * P], uph[:, t % 2, 0:KT * P].bitcast(F32), ALU.subtract).then_inc(up_lo, 1)
                    if t >= 3:
                        add_square(t - 2)
                add_square(6)
                lo_up(0, 0)
                add_square(7)
                lo_up(1, 1)
                lo_down(0)
                lo_up(2, 0)
                with pool.Fori(1, GROUPS - 1) as i:
                    lo_up(i * 2 + 1, 1)
                    lo_up(i * 2 + 2, 0)
                    lo_down(i)
                lo_up(FT - 1, 1)
                lo_down(GROUPS - 1)
                add_squares(l * 16 + 16, l * 14 + 14, sq3[:, :])
                meet(pool, l, 3)
            step.leave(was, "pool layer", L)

        @block.scalar
        def _(act):
            def gained(t, gain, final):
                act.wait_ge(*final)
                act.activation(xgh[:, t, :], xT[:, t, :], ACT.Identity, scale=gain[:, t:t + 1]).then_inc(xg_hi, 1)

            def square(t, final, s0, buf):
                act.wait_ge(*final)
                if t > 1:
                    act.wait_ge(sq_added, s0 + t - 1)
                act.activation(rstd[:, :] if t == 0 else buf, xT[:, t, :], ACT.Square).then_inc(x_squared, 1)

            act.wait_ge(const_loaded, 32)
            for t in range(KT):
                gained(t, gain0, (x_final, t + 1))
                square(t, (x_final, t + 1), 0, sq[:, :])
            meet(act, 0, 0)

            with act.Fori(0, L) as l:
                def hi_item(n):
                    it = ITEMS[n]
                    act.wait_ge(wraw_full[n % 2], (l * RAWS[n % 2] + raw_dmas(n)) * 16)
                    w = wraw[:, n % 2, :]
                    if it == "uq":
                        act.activation(wqh[:, 0, :], w[:, 0:384], ACT.Copy)
                        act.activation(wqh[0:64, 1, :], w[0:64, 384:768], ACT.Copy).then_inc(w_hi, 1)
                    elif it == "ukv":
                        act.activation(wkh[:, :], w[:, 0:512], ACT.Copy).then_inc(w_hi, 1)
                    else:
                        if it >= 2:
                            act.wait_ge(proj_done, l * NT + it - 1)
                        act.activation(wh[:, it % 2, :], w, ACT.Copy).then_inc(w_hi, 1)

                def root(j, dst, scale):
                    act.activation(two(dst), ps[:, 4 + 2 * (j % 2):6 + 2 * (j % 2), :], ACT.Sqrt, bias=eps, scale=scale).then_inc(job_free, 1)

                def job(kind, a):
                    j = job_no(kind, a)
                    if kind in ("scq", "sckv", "sa"):
                        act.wait_ge(sq_free, l * len(SQUARED) + {"scq": 2, "sckv": 3}.get(kind, a))
                    else:
                        act.wait_ge(job_ready, l * NR + ready_no(kind, a) + 1)
                    src = ps[:, 4 + 2 * (j % 2):6 + 2 * (j % 2), :]
                    if kind in ("sx", "scq", "sckv", "sa"):
                        if kind == "scq":
                            act.wait_ge(r_free, l + 1)
                        elif kind == "sckv":
                            act.wait_ge(latent_ready, l * 2 + 1)
                        elif kind == "sa" and a == 4:
                            act.wait_ge(roped, l * NB + NB)
                        elif kind == "sa":
                            act.wait_ge(out_ready, l * 6 + a - 3)
                        root(j, r[:, :], {"sx": 1.0 / D, "scq": 1.0 / QR, "sckv": 1.0 / KVR, "sa": 1.0 / HD}[kind])
                    elif kind == "uq":
                        if a >= 2:
                            act.wait_ge(e_stored[a % 2], l * 64 + 16)
                        act.activation(two(e[0:96, a % 2, :]), src[0:96], ACT.Copy).then_inc(job_free, 1)
                    elif kind == "ukv":
                        act.wait_ge(e_stored[a % 2], l * 64 + 16 * (2 + a // 2))
                        if a >= 2:
                            act.wait_ge(job_ready, l * NR + ready_no("tr", a - 2) + 1)
                        act.activation(two(e[:, a % 2, :]), src, ACT.Copy).then_inc(job_free, 1)
                    else:
                        n = [x for x in JOB_LIST if x[0] in ("tr", "tv")].index((kind, a))
                        if n:
                            act.wait_ge(vt_stored, l * (7 * 16) + 16 * n)
                        s4 = src.rearrange("p b (m c) -> p (b m) c", m=4)
                        if kind == "tr":
                            act.activation(vt[:, :, 0:HD], s4[:, :, HD:P], ACT.Copy).then_inc(job_free, 1)
                        else:
                            act.activation(vt[:, :, :], s4, ACT.Copy).then_inc(job_free, 1)

                hi_item(0)
                hi_item(1)
                nxt = 2
                for t in range(NT):
                    while nxt < NI and nxt <= item_no(t) + 2:
                        hi_item(nxt)
                        nxt += 1
                    for kind, a in JOBS.get(t, []):
                        job(kind, a)
                    if t in SQUARED:
                        act.wait_ge(z_ready, l * NT + t + 1)
                        n = SQUARED.index(t)
                        if n:
                            act.wait_ge(sq_free, l * len(SQUARED) + n)
                        act.activation(sq[:, :], z[:, t % 2, :], ACT.Square).then_inc(sq_ready, 1)
                meet(act, l, 1)

                act.activation(small[:, 2:4], small[:, 0:2], ACT.Exp).then_inc(lam_exp, 1)

                def exp_item(x, i):
                    it, b = x["item0"] + i, x["half"]
                    act.wait_ge(max_done, l * NS + it + 1)
                    if x["group"] == "C":
                        dst = prob1[:, :] if i % 2 else prob[:, b, i // 2, :]
                        if i % 2:
                            n = 4 * (x["u"] - U_C) + i // 2
                            if n:
                                act.wait_ge(mixed, l * 32 + n)
                        scale = SLOPES[x["h"]]
                    else:
                        dst, scale = prob[:, b, i, :], (SCALE_A if x["group"] == "A" else SCALE_B)
                    act.activation(two(dst), ps[:, 2 * (i % 2):2 * (i % 2) + 2, :], ACT.Exp, bias=nmx[:, b, i:i + 1],
                                   scale=scale, accum_out=rsum[:, b, i:i + 1]).then_inc(exp_done, 1)

                def act_unit(x, nx):
                    for s in range(8):
                        act.wait_ge(trans_done, l * (8 * NU) + x["u"] * 8 + s + 1)
                        act.wait_ge(av_done, l * (8 * NU) + x["u"] * 8 + s + 1 - NPT + AV_CREDIT)
                        act.activation(pth[:, s % NPT, :], ps[:, 4 + s % 2, :], ACT.Copy).then_inc(pt_hi, 1)
                        i = STEP_OF[nx["items"]].get(s) if nx else None
                        if i is not None:
                            exp_item(nx, i)
                    act.wait_ge(av_done, l * (8 * NU) + x["u"] * 8 + 8 + AV_CREDIT)
                    act.activation(obot[:, :], ps[HD:P, 6, :], ACT.Copy).then_inc(bot_copied, 1)
                    if x["group"] != "C":
                        act.wait_ge(o_ready, l * U_C + x["u"] + 1 + O_CREDIT)
                        act.activation(mix_at(xgh, x), osum[:, :], ACT.Copy).then_inc(mix_hi, 1)

                for i in range(4):
                    exp_item(unit("A", 0, 0), i)
                run_pairs(act, act_unit)
                meet(act, l, 2)

                def hi_out(t):
                    act.wait_ge(up_full, (l * (KT + 2 * FT) + t + 1) * 16)
                    if t >= 2:
                        act.wait_ge(op_done, l * KT + t - 1)
                    act.activation(uph[:, t % 2, 0:KT * P], upraw[:, 0:KT * P], ACT.Copy).then_inc(up_hi, 1)

                def hi_up(f, par):
                    act.wait_ge(up_full, (l * (KT + 2 * FT) + f * 2 + KT + 2) * 16)
                    if isinstance(f, int) and f < 2:
                        act.wait_ge(op_done, l * KT + KT - 1 + f)
                    else:
                        act.wait_ge(up_done, l * FT + f - 1)
                    act.activation(uph[:, par, :], upraw[:, :], ACT.Copy).then_inc(up_hi, 1)

                def hi_down(g):
                    act.wait_ge(dn_full, (l * GROUPS + g + 1) * 16)
                    if not (isinstance(g, int) and g == 0):
                        act.wait_ge(down_done, l * (16 * GROUPS) + g * 16)
                    act.activation(dnh[:, :, :], draw[:, :, :], ACT.Copy).then_inc(dn_hi, 1)

                for c in range(2):
                    act.activation(cv[:, c, :], oc[:, c, :], ACT.Square).then_inc(c_squared, 1)
                hi_out(0)
                for c in range(2):
                    act.wait_ge(c_stat, l * 2 + c + 1)
                    act.activation(two(cv[:, c, :]), ps[:, 4 + 2 * c:6 + 2 * c, :], ACT.Sqrt, bias=eps, scale=1.0 / HD).then_inc(c_root, 1)
                hi_out(1)
                for c in range(2):
                    act.wait_ge(c_normed, l * 2 + c + 1)
                    act.activation(xgh[:, 6 + c, :], cv[:, c, :], ACT.Copy).then_inc(c_hi, 1)
                for t in range(2, KT):
                    hi_out(t)
                    square(t - 2, (x_final, l * KT + KT + t - 2 + 1), l * 14 + 7, sq3[:, :])
                hi_up(0, 0)
                square(6, (x_final, l * KT + KT + 6 + 1), l * 14 + 7, sq3[:, :])
                act.wait_ge(vec_loaded, l * 16 + 16)
                act.wait_ge(op_done, l * KT + KT)
                for t in range(KT):
                    gained(t, vec[:, V_FFN:V_FFN + KT], (x_final, l * KT + KT + t + 1))
                square(7, (x_final, l * KT + KT + 7 + 1), l * 14 + 7, sq3[:, :])
                hi_up(1, 1)
                act.wait_ge(stat_done, l + 1)
                act.activation(two(sq3[:, :]), ps[:, 4:6, :], ACT.Sqrt, bias=eps, scale=1.0 / D).then_inc(root_done, 1)
                hi_down(0)

                def mid_taps(f):
                    act.wait_ge(u_ready, l * FT + f + 1)
                    if not (isinstance(f, int) and f == 0):
                        act.wait_ge(a_lo, l * FT + f)
                    for c in range(2):
                        ins = act.activation(cv[:, c, :], u[:, c, 1:T + 1], ACT.Identity,
                                             scale=vec[:, bass.ds(f + (V_CONV + 2 * FT + c * FT), 1)],
                                             bias=vec[:, bass.ds(f + (V_CONV + 6 * FT + c * FT), 1)])
                    ins.then_inc(tap_mid, 1)

                def gate(f):
                    act.wait_ge(conv_done, l * FT + f + 1)
                    act.activation(cv[:, 0, :], cv[:, 0, :], ACT.Silu).then_inc(silu_done, 1)

                def hi_a(f, par):
                    act.wait_ge(prod_done, l * FT + f + 1)
                    if not (isinstance(f, int) and f < 2):
                        act.wait_ge(down_done, l * (16 * GROUPS) + (f - par) * 8)
                    act.activation(ah[:, par, :], cv[:, 0, :], ACT.Copy).then_inc(a_hi, 1)

                mid_taps(0)
                hi_up(2, 0)
                gate(0)
                hi_a(0, 0)
                mid_taps(1)
                gate(1)
                hi_a(1, 1)

                def act_group(i, last):
                    mid_taps(i * 2)
                    hi_up(i * 2 + 1, 1)
                    gate(i * 2)
                    if not last:
                        hi_up(i * 2 + 2, 0)
                    hi_a(i * 2, 0)
                    hi_down(i)
                    mid_taps(i * 2 + 1)
                    gate(i * 2 + 1)
                    hi_a(i * 2 + 1, 1)

                with act.Fori(1, GROUPS - 1) as i:
                    act_group(i, False)
                act_group(GROUPS - 1, True)
                for t in range(KT):
                    final = (y_done, (l + 1) * (16 * GROUPS) - 16 + 2 * t + 2)
                    gained(t, vec[:, V_NEXT:V_NEXT + KT], final)
                    square(t, final, l * 14 + 14, sq3[:, :])
                meet(act, l, 3)

            act.wait_ge(stat_done, L + 1)
            act.activation(two(r[:, :]), ps[:, 4:6, :], ACT.Sqrt, bias=eps, scale=1.0 / D).then_inc(root_done, 1)
            for t in range(KT):
                act.wait_ge(fin_trans, t + 1)
                if t >= 2:
                    act.wait_ge(out_stored[t % 2], 16 * (t // 2))
                act.activation(two(e[:, t % 2, :]), ps[:, 2 * (t % 2):2 * (t % 2) + 2, :], ACT.Copy).then_inc(fin_copied, 1)

        @block.vector
        def _(dve):
            step = Steps(dve, dve_step)
            for s, n in ((pt_lo, PT_CREDIT), (exp_done, EXP_CREDIT), (av_done, AV_CREDIT), (o_read, O_CREDIT), (o_ready, O_CREDIT)):
                for c in range(n):
                    dve.memset(small[64:65, 6:7], 0.0).then_inc(s, 1)
                    dve.wait_ge(s, c + 1)

            def lo_gained(t, n, gain):
                dve.wait_ge(xg_hi, n)
                dve.scalar_tensor_tensor(xgl[:, t, :], xT[:, t, :], gain[:, t:t + 1], xgh[:, t, :].bitcast(F32),
                                         ALU.mult, ALU.subtract).then_inc(xg_lo, 1)

            dve.wait_ge(const_loaded, 32)
            for t in range(KT):
                dve.wait_ge(xt_done, t + 1)
                dve.tensor_copy(two(xT[:, t, :]), ps[:, 2 * (t % 2):2 * (t % 2) + 2, :]).then_inc(x_final, 1)
                if t:
                    lo_gained(t - 1, t, gain0)
            lo_gained(KT - 1, KT, gain0)
            meet(dve, 0, 0)

            with dve.Fori(0, L) as l:
                was = step.enter(l, "dve layer")

                def evacuate(t):
                    dve.wait_ge(proj_done, l * NT + t + 1)
                    zz = z[:, t % 2, :]
                    if t >= 2 and t - 2 in Z_OUT:
                        dve.wait_ge(z_stored[t % 2], (l * ZS[t % 2] + z_stores(t - 2)) * 16)
                    if t == 15:
                        dve.wait_ge(job_ready, l * NR + ready_no("tv", 13) + 1)
                    for b in range(2):
                        src, dst, rs = ps[:, 2 * (t % 2) + b, :], zz[:, b * HALF:(b + 1) * HALF], rstd[:, b * HALF:(b + 1) * HALF]
                        if t in (9, 10, 11, 12):
                            ins = dve.scalar_tensor_tensor(dst, src, cst[:, C_SC + t - 9:C_SC + t - 8], rs, ALU.mult, ALU.mult)
                        else:
                            ins = dve.tensor_tensor(dst, src, rs, ALU.mult)
                    ins.then_inc(z_ready, 1)
                    dve.wait_ge(z_ready, l * NT + t + 1)

                def rope(v, tab, r0, r1, shift):
                    mask = [j // (2 * shift) * 2 * shift + (j + shift) % (2 * shift) for j in range(32)]
                    settle(dve)
                    step(dve.stream_shuffle(r[r0:r1, :], v[r0:r1, :], mask))
                    step(dve.tensor_tensor(r[r0:r1, :], r[r0:r1, :], tab[r0:r1, 1, :], ALU.mult))
                    step(dve.tensor_tensor(v[r0:r1, :], v[r0:r1, :], tab[r0:r1, 0, :], ALU.mult))
                    return dve.tensor_tensor(v[r0:r1, :], v[r0:r1, :], r[r0:r1, :], ALU.add)

                def latent(t, slot, gain, rows):
                    zz = z[0:rows, t % 2, :]
                    step(dve.scalar_tensor_tensor(zz, zz, gain, r[0:rows, :], ALU.mult, ALU.mult))
                    step(dve.tensor_copy(ch[0:rows, slot, :], zz))
                    return dve.tensor_tensor(cl[0:rows, slot, :], zz, ch[0:rows, slot, :].bitcast(F32), ALU.subtract)

                def wait_root(kind, a=0):
                    dve.wait_ge(job_free, l * NJ + job_no(kind, a) + 1)

                def per_head(t):
                    wait_root("sa", t)
                    zz = z[:, t % 2, :]
                    g = V_QG if t < 8 else V_KG
                    step(dve.reciprocal(r[:, :], r[:, :]))
                    step(dve.scalar_tensor_tensor(zz, zz, vec[:, g:g + 1], r[:, :], ALU.mult, ALU.mult))
                    rope(zz, ra, 0, P, 16).then_inc(out_ready, 1)
                    dve.wait_ge(out_ready, l * 6 + t - 2)

                wait_root("sx")
                dve.reciprocal(rstd[:, :], r[:, :]).then_inc(r_free, 1)
                dve.wait_ge(r_free, l + 1)
                evacuate(0)
                evacuate(1)
                dve.wait_ge(vec_loaded, l * 16 + 16)
                for i in range(2):
                    a, b = V_LAM + 2 * i * CQK, V_LAM + (2 * i + 1) * CQK
                    step(dve.tensor_tensor(vec[:, a:a + CQK], vec[:, a:a + CQK], vec[:, b:b + CQK], ALU.mult))
                    step(dve.tensor_reduce(small[:, i:i + 1], vec[:, a:a + CQK], AX.X, ALU.add))
                step(dve.tensor_tensor(small[:, 5:6], vec[:, V_SUB:V_SUB + 1], vec[:, V_LI + 1:V_LI + 2], ALU.mult))
                wait_root("scq")
                step(dve.reciprocal(r[:, :], r[:, :]))
                step(latent(0, 0, vec[:, V_CQG:V_CQG + 1], P))
                latent(1, 1, vec[0:64, V_CQG + 1:V_CQG + 2], 64).then_inc(latent_ready, 1)
                dve.wait_ge(latent_ready, l * 2 + 1)
                evacuate(2)
                evacuate(3)
                wait_root("sckv")
                step(dve.reciprocal(r[:, :], r[:, :]))
                latent(2, 2, vec[:, V_CKVG:V_CKVG + 1], P).then_inc(latent_ready, 1)
                dve.wait_ge(latent_ready, l * 2 + 2)
                dve.wait_ge(rope_loaded, (l + 1) * 6 * 16)
                rope(z[:, 1, :], rb_, 0, ROPE, 8).then_inc(out_ready, 1)
                dve.wait_ge(out_ready, l * 6 + 1)
                evacuate(4)
                for h in range(NB):
                    dve.wait_ge(job_free, l * NJ + job_no("uq", h) + 1)
                    rope(e[:, h % 2, :], rb_, NOPE, 96, 8).then_inc(roped, 1)
                    dve.wait_ge(roped, l * NB + h + 1)
                for t in range(5, NT):
                    evacuate(t)
                    if 4 <= t - 1 <= 8:
                        per_head(t - 1)
                meet(dve, l, 1)

                dve.wait_ge(lam_exp, l + 1)
                step(dve.tensor_tensor(small[:, 4:5], small[:, 3:4], small[:, 2:3], ALU.subtract))
                step(dve.tensor_tensor(small[:, 4:5], small[:, 4:5], vec[:, V_LI:V_LI + 1], ALU.subtract))
                dve.wait_ge(dtab_loaded, l * 16 + 16)

                def max_item(x, i):
                    b = x["half"]
                    dve.wait_ge(scores_done, l * NS + x["item0"] + i + 1)
                    src = ps[:, 2 * (i % 2):2 * (i % 2) + 2, :]
                    if x["group"] == "C":
                        off = T - P - P * (4 * b + i // 2)
                        scale = SLOPES[x["h"]]
                        settle(dve)
                        step(dve.tensor_tensor_reduce(src, src, two(dtab[:, off:off + T]), 1.0, -3.0e38, ALU.subtract, ALU.max, mx[:, b, i:i + 1]))
                    else:
                        scale = SCALE_A if x["group"] == "A" else SCALE_B
                        step(dve.tensor_reduce(mx[:, b, i:i + 1], src, AX.XY, ALU.max))
                    dve.tensor_scalar(nmx[:, b, i:i + 1], mx[:, b, i:i + 1], -scale, None, ALU.mult).then_inc(max_done, 1)

                def mix_maps(x, i):
                    b = x["half"]
                    dve.wait_ge(exp_done, l * NS + x["item0"] + 2 * i + 2 + EXP_CREDIT)
                    step(dve.reciprocal(rinv[:, b, 2 * i:2 * i + 2], rsum[:, b, 2 * i:2 * i + 2]))
                    step(dve.tensor_tensor(rinv[:, b, 2 * i + 1:2 * i + 2], rinv[:, b, 2 * i + 1:2 * i + 2], small[:, 4:5], ALU.mult))
                    step(dve.tensor_scalar(prob1[:, :], prob1[:, :], rinv[:, b, 2 * i + 1:2 * i + 2], None, ALU.mult))
                    dve.scalar_tensor_tensor(prob[:, b, i, :], prob[:, b, i, :], rinv[:, b, 2 * i:2 * i + 1], prob1[:, :],
                                             ALU.mult, ALU.add).then_inc(mixed, 1)

                def dve_unit(x, nx):
                    b = x["half"]
                    for s in range(8):
                        i = STEP_OF[nx["items"]].get(s) if nx else None
                        if i is not None:
                            max_item(nx, i)
                        dve.wait_ge(pt_hi, l * (8 * NU) + x["u"] * 8 + s + 1)
                        k = s % NPT
                        dve.tensor_tensor(ptl[:, k, :], ps[:, 4 + s % 2, :], pth[:, k, :].bitcast(F32), ALU.subtract).then_inc(pt_lo, 1)
                        if s == 1 and x["group"] != "C":
                            dve.wait_ge(exp_done, l * NS + x["item0"] + 4 + EXP_CREDIT)
                            step(dve.reciprocal(rinv[:, b, 0:4], rsum[:, b, 0:4]))
                            for m in range(4):
                                ins = dve.tensor_scalar(diag[:, m, :], ident, rinv[:, b, m:m + 1], None, ALU.mult)
                            ins.then_inc(diag_done, 1)
                        if nx and nx["group"] == "C" and s >= 2 and s % 2 == 0:
                            mix_maps(nx, s // 2 - 1)
                    dve.wait_ge(bot_copied, l * NU + x["u"] + 1)
                    if x["group"] != "C":
                        dve.tensor_tensor(osum[:, :], ps[0:HD, 6, :], obot[:, :], ALU.add).then_inc(o_read, 1)
                        dve.wait_ge(o_read, l * NU + x["u"] + 1 + O_CREDIT)
                        dve.wait_ge(norm_done, l * U_C + x["u"] + 1)
                        dve.tensor_tensor(osum[:, :], osum[:, :], ps[0:HD, 7, :], ALU.mult).then_inc(o_ready, 1)
                        dve.wait_ge(mix_hi, l * U_C + x["u"] + 1)
                        lo_mix(x)
                    else:
                        h = x["h"]
                        dst = oc[HD * (h % 2):HD * (h % 2) + HD, h // 2, b * HALF:(b + 1) * HALF]
                        dve.tensor_tensor(dst, ps[0:HD, 6, :], obot[:, :], ALU.add).then_inc(o_read, 1)
                    if nx and nx["group"] == "C":
                        mix_maps(nx, 3)

                def lo_mix(x):
                    step(dve.tensor_copy(ohi[:, :], osum[:, :]))
                    dve.tensor_tensor(mix_at(xgl, x), osum[:, :], ohi[:, :].bitcast(F32), ALU.subtract).then_inc(mix_lo, 1)

                for i in range(4):
                    max_item(unit("A", 0, 0), i)
                run_pairs(dve, dve_unit, step)
                meet(dve, l, 2)

                for c in range(2):
                    dve.wait_ge(c_root, l * 2 + c + 1)
                    step(dve.reciprocal(cv[:, c, :], cv[:, c, :]))
                    dve.scalar_tensor_tensor(cv[:, c, :], oc[:, c, :], small[:, 5:6], cv[:, c, :], ALU.mult, ALU.mult).then_inc(c_normed, 1)
                for c in range(2):
                    dve.wait_ge(c_hi, l * 2 + c + 1)
                    dve.tensor_tensor(xgl[:, 6 + c, :], cv[:, c, :], xgh[:, 6 + c, :].bitcast(F32), ALU.subtract).then_inc(c_lo, 1)
                step(dve.memset(u[:, :, 0:1], 0.0))
                step(dve.memset(u[:, :, T + 1:T + 2], 0.0))
                for t in range(KT):
                    dve.wait_ge(op_done, l * KT + t + 1)
                    dve.wait_ge(x_back[t], l * 16 + 16)
                    dve.tensor_tensor(two(xT[:, t, :]), ps[:, 2 * (t % 2):2 * (t % 2) + 2, :], two(xT[:, t, :]), ALU.add).then_inc(x_final, 1)
                for t in range(KT):
                    lo_gained(t, l * 16 + 8 + t + 1, vec[:, V_FFN:V_FFN + KT])
                dve.wait_ge(root_done, l + 1)
                dve.reciprocal(rstd[:, :], sq3[:, :]).then_inc(rstd_done, 1)
                dve.wait_ge(rstd_done, l + 1)

                def conv_in(f, par):
                    dve.wait_ge(up_done, l * FT + f + 1)
                    for c in range(2):
                        for b in range(2):
                            ins = dve.tensor_tensor(u[:, c, 1 + b * HALF:1 + (b + 1) * HALF], ps[:, 4 * par + 2 * c + b, :],
                                                    rstd[:, b * HALF:(b + 1) * HALF], ALU.mult)
                    ins.then_inc(u_ready, 1)
                    dve.wait_ge(u_ready, l * FT + f + 1)

                def tap(f, c, k):
                    return dve.scalar_tensor_tensor(cv[:, c, :], u[:, c, k:k + T], vec[:, bass.ds(f + (V_CONV + 2 * k * FT + c * FT), 1)],
                                                    cv[:, c, :], ALU.mult, ALU.add)

                def outer_taps(f, c):
                    if c == 0:
                        dve.wait_ge(tap_mid, l * FT + f + 1)
                    step(tap(f, c, 0))
                    if c == 0:
                        tap(f, c, 2).then_inc(conv_done, 1)
                    else:
                        step(tap(f, c, 2))

                def gate_value(f):
                    dve.wait_ge(silu_done, l * FT + f + 1)
                    dve.tensor_tensor(cv[:, 0, :], cv[:, 0, :], cv[:, 1, :], ALU.mult).then_inc(prod_done, 1)

                def lo_a(f, par):
                    dve.wait_ge(a_hi, l * FT + f + 1)
                    dve.tensor_tensor(al[:, par, :], cv[:, 0, :], ah[:, par, :].bitcast(F32), ALU.subtract).then_inc(a_lo, 1)

                def add_down(g, j):
                    t, b = j // 2, j % 2
                    dve.wait_ge(down_done, l * (16 * GROUPS) + g * 16 + j + 1)
                    xs = xT[:, t, b * HALF:(b + 1) * HALF]
                    ins = dve.tensor_tensor(xs, ps[:, 4 + j % 4, :], xs, ALU.add)
                    ins.then_inc(y_done, 1)

                for f in range(2):
                    conv_in(f, f)
                    outer_taps(f, 0)
                    outer_taps(f, 1)
                    gate_value(f)
                    lo_a(f, f)

                def dve_group(i):
                    g = i - 1
                    conv_in(i * 2, 0)
                    for j in range(16):
                        add_down(g, j)
                        if j == 3:
                            outer_taps(i * 2, 0)
                        if j == 6:
                            outer_taps(i * 2, 1)
                        if j == 9:
                            gate_value(i * 2)
                    lo_a(i * 2, 0)
                    conv_in(i * 2 + 1, 1)
                    outer_taps(i * 2 + 1, 0)
                    outer_taps(i * 2 + 1, 1)
                    gate_value(i * 2 + 1)
                    lo_a(i * 2 + 1, 1)

                with dve.Fori(1, GROUPS) as i:
                    w2 = step.enter(i, "dve group", 1)
                    dve_group(i)
                step.leave(w2, "dve group", GROUPS - 1)
                for j in range(16):
                    add_down(GROUPS - 1, j)
                    if j % 2:
                        dve.wait_ge(y_done, l * (16 * GROUPS) + 16 * (GROUPS - 1) + j + 1)
                        if j > 2:
                            lo_gained(j // 2 - 1, l * 16 + 16 + j // 2, vec[:, V_NEXT:V_NEXT + KT])
                lo_gained(KT - 1, l * 16 + 24, vec[:, V_NEXT:V_NEXT + KT])
                meet(dve, l, 3)
            step.leave(was, "dve layer", L)

            dve.wait_ge(root_done, L + 1)
            dve.reciprocal(rstd[:, :], r[:, :]).then_inc(rstd_done, 1)
            dve.wait_ge(rstd_done, L + 1)
            for t in range(KT):
                if t >= 2:
                    dve.wait_ge(fin_trans, t - 1)
                dve.scalar_tensor_tensor(z[:, t % 2, :], xT[:, t, :], vec[:, V_NEXT + t:V_NEXT + t + 1], rstd[:, :], ALU.mult, ALU.mult).then_inc(fin_ready, 1)

        @block.tensor
        def _(pe):
            pe.wait_ge(const_loaded, 32)
            for t in range(KT):
                if t == 0:
                    pe.wait_ge(x_loaded, 16 * TT)
                if t >= 2:
                    pe.wait_ge(x_final, t - 1)
                for m in range(TT):
                    ins = pe.transpose(ps[:, 2 * (t % 2) + m // 4, (m % 4) * P:(m % 4 + 1) * P], stage[m][:, t * P:(t + 1) * P], ident)
                ins.then_inc(xt_done, 1)
            meet(pe, 0, 0)

            def three(outs, wh_, wl_, xh, xl, start, stop):
                for n, (a, x_) in enumerate(((wh_, xh), (wl_, xh), (wh_, xl))):
                    for b in range(2):
                        ins = pe.matmul(outs[b], a, x_[:, b * HALF:(b + 1) * HALF], start=start and n == 0, stop=stop and n == 2)
                return ins

            with pe.Fori(0, L) as l:
                def project(t):
                    pe.wait_ge(w_lo, l * NI + item_no(t) + 1)
                    if t >= 2:
                        pe.wait_ge(z_ready, l * NT + t - 1)
                    if t == 0:
                        pe.wait_ge(xg_lo, l * 16 + 8)
                    outs = [ps[:, 2 * (t % 2) + b, :] for b in range(2)]
                    for k in range(KT):
                        ins = three(outs, wh[:, t % 2, k * P:(k + 1) * P], wl[:, t % 2, k * P:(k + 1) * P],
                                    xgh[:, k, :], xgl[:, k, :], k == 0, k == KT - 1)
                    ins.then_inc(proj_done, 1)

                def bank(j, b):
                    return ps[:, 4 + 2 * (j % 2) + b, :]

                def squares_sum(j, n, lhsT, src, start, stop):
                    pe.wait_ge(sq_ready, l * len(SQUARED) + n + 1)
                    for b in range(2):
                        ins = pe.matmul(bank(j, b), lhsT, src[:, b * HALF:(b + 1) * HALF], start=start, stop=stop)
                    return ins

                def job(kind, a):
                    j = job_no(kind, a)
                    if j >= 2:
                        pe.wait_ge(job_free, l * NJ + j - 1)
                    if kind == "sx":
                        pe.wait_ge(sq_added, l * 14 + 7)
                        for b in range(2):
                            ins = pe.matmul(bank(j, b), ones, rstd[:, b * HALF:(b + 1) * HALF], start=True, stop=True)
                    elif kind == "scq":
                        squares_sum(j, 1, ones[0:64, :], sq[0:64, :], False, True).then_inc(sq_free, 1)
                        ins = None
                    elif kind in ("sckv", "sa"):
                        n = 2 if kind == "sckv" else a - 1
                        squares_sum(j, n, ones if kind == "sckv" else blk, sq[:, :], True, True).then_inc(sq_free, 1)
                        ins = None
                    elif kind == "uq":
                        if a == 0:
                            pe.wait_ge(w_lo, l * NI + item_no("uq") + 1)
                            pe.wait_ge(latent_ready, l * 2 + 1)
                        outs = [ps[0:96, 4 + 2 * (j % 2) + b, :] for b in range(2)]
                        for k, rows in ((0, P), (1, QR - P)):
                            ins = three(outs, wqh[0:rows, k, a * 96:(a + 1) * 96], wql[0:rows, k, a * 96:(a + 1) * 96],
                                        ch[0:rows, k, :], cl[0:rows, k, :], k == 0, k == 1)
                    elif kind == "ukv":
                        if a == 0:
                            pe.wait_ge(w_lo, l * NI + item_no("ukv") + 1)
                            pe.wait_ge(latent_ready, l * 2 + 2)
                        ins = three([bank(j, 0), bank(j, 1)], wkh[:, a * P:(a + 1) * P], wkl[:, a * P:(a + 1) * P],
                                    ch[:, 2, :], cl[:, 2, :], True, True)
                    else:
                        if kind == "tr":
                            pe.wait_ge(job_free, l * NJ + job_no("ukv", a) + 1)
                            src = e[:, a % 2, :]
                        else:
                            pe.wait_ge(z_ready, l * NT + a + 1)
                            src = z[:, a % 2, :]
                        for m in range(TT):
                            ins = pe.transpose(ps[:, 4 + 2 * (j % 2) + m // 4, (m % 4) * P:(m % 4 + 1) * P], src[:, m * P:(m + 1) * P], ident)
                    if ins is not None:
                        ins.then_inc(job_ready, 1)

                for t in range(NT):
                    project(t)
                    if t == 1:
                        squares_sum(job_no("scq", 0), 0, ones, sq[:, :], True, False).then_inc(sq_free, 1)
                    for kind, a in JOBS.get(t, []):
                        job(kind, a)
                meet(pe, l, 1)

                def score_item(x, i):
                    it, st, b = x["item0"] + i, stack[x["par"]], x["half"]
                    if i == 0 and x["half"] == 0:
                        pe.wait_ge(vraw_free, l * (NA + NB + NC) + x["h"] + HEAD0[x["group"]] + 2)
                    pe.wait_ge(exp_done, l * NS + it - 1 + EXP_CREDIT)
                    qt = i // 2 if x["group"] == "C" else i
                    c0 = b * HALF + qt * P
                    if x["group"] == "A":
                        rows, terms = P, ((0, 1), (0, 2))
                    elif x["group"] == "B":
                        rows, terms = 96, ((0, 2), (1, 2), (0, 3))
                    else:
                        rows, terms = P, ((2 * (i % 2), 2 * (i % 2) + 1),)
                    for n, (q, k) in enumerate(terms):
                        for kh in range(2):
                            ins = pe.matmul(ps[:, 2 * (i % 2) + kh, :], st[q][0:rows, c0:c0 + P], st[k][0:rows, kh * HALF:(kh + 1) * HALF],
                                            start=n == 0, stop=n == len(terms) - 1)
                    ins.then_inc(scores_done, 1)

                def pe_unit(x, nx):
                    b, v = x["half"], vst[x["par"]]
                    if x["group"] == "C":
                        pe.wait_ge(mixed, l * 32 + 4 * (x["u"] - U_C) + 4)
                    else:
                        pe.wait_ge(exp_done, l * NS + x["item0"] + 4 + EXP_CREDIT)

                    def value_product(s):
                        if s == 0:
                            pe.wait_ge(o_read, l * NU + x["u"] + O_CREDIT)
                        pe.wait_ge(pt_lo, l * (8 * NU) + x["u"] * 8 + s + 1 + PT_CREDIT)
                        k = s % NPT
                        pe.matmul(ps[:, 6, :], v[:, s, :], pth[:, k, :], start=s == 0, stop=False)
                        pe.matmul(ps[:, 6, :], v[:, s, :], ptl[:, k, :], start=False, stop=s == 7).then_inc(av_done, 1)

                    for s in range(8):
                        i = STEP_OF[nx["items"]].get(s) if nx else None
                        if i is not None:
                            score_item(nx, i)
                        pe.wait_ge(pt_lo, l * (8 * NU) + x["u"] * 8 + s - 1 + PT_CREDIT)
                        for m in range(4):
                            ins = pe.transpose(ps[:, 4 + s % 2, m * P:(m + 1) * P], prob[:, b, m, s * P:(s + 1) * P], ident)
                        ins.then_inc(trans_done, 1)
                        if s >= LAG:
                            value_product(s - LAG)
                        if s == 4 and x["group"] != "C":
                            pe.wait_ge(diag_done, l * U_C + x["u"] + 1)
                            pe.wait_ge(o_ready, l * U_C + x["u"] + O_CREDIT)
                            pe.matmul(ps[:, 7, :], ones, diag[:, :, :].rearrange("p m n -> p (m n)"), start=True, stop=True).then_inc(norm_done, 1)
                    for s in range(8 - LAG, 8):
                        value_product(s)

                for i in range(4):
                    score_item(unit("A", 0, 0), i)
                run_pairs(pe, pe_unit)
                meet(pe, l, 2)

                for c in range(2):
                    pe.wait_ge(c_squared, l * 2 + c + 1)
                    for b in range(2):
                        ins = pe.matmul(ps[:, 4 + 2 * c + b, :], blk, cv[:, c, b * HALF:(b + 1) * HALF], start=True, stop=True)
                    ins.then_inc(c_stat, 1)
                for t in range(KT):
                    pe.wait_ge(up_lo, l * (KT + FT) + t + 1)
                    if t >= 2:
                        pe.wait_ge(x_final, l * KT + KT + t - 1)
                    outs = [ps[:, 2 * (t % 2) + b, :] for b in range(2)]
                    for k in range(KT):
                        if t == 0 and k >= 6:
                            pe.wait_ge(c_lo, l * 2 + k - 5)
                        ins = three(outs, uph[:, t % 2, k * P:(k + 1) * P], upl[:, t % 2, k * P:(k + 1) * P],
                                    xgh[:, k, :], xgl[:, k, :], k == 0, k == KT - 1)
                    ins.then_inc(op_done, 1)

                def up(f, par):
                    pe.wait_ge(up_lo, l * (KT + FT) + KT + f + 1)
                    first = isinstance(f, int)
                    if first and f == 0:
                        pe.wait_ge(x_final, l * KT + KT + KT)
                    elif first and f == 1:
                        pe.wait_ge(root_done, l + 1)
                    elif par == 0:
                        pe.wait_ge(u_ready, l * FT + f - 1)
                    else:
                        pe.wait_ge(y_done, l * (16 * GROUPS) + f * 8 - 8)
                    for k in range(KT):
                        if first and f == 0:
                            pe.wait_ge(xg_lo, l * 16 + 8 + k + 1)
                        for c in range(2):
                            o = (2 * k + c) * P
                            outs = [ps[:, 4 * par + 2 * c + b, :] for b in range(2)]
                            ins = three(outs, uph[:, par, o:o + P], upl[:, par, o:o + P], xgh[:, k, :], xgl[:, k, :], k == 0, k == KT - 1)
                    ins.then_inc(up_done, 1)

                def down(g):
                    pe.wait_ge(dn_lo, l * GROUPS + g + 1)
                    pe.wait_ge(a_lo, l * FT + g * 2 + 2)
                    for j in range(16):
                        t, b = j // 2, j % 2
                        if j >= 4:
                            pe.wait_ge(y_done, l * (16 * GROUPS) + g * 16 + j - 3)
                        for n in range(6):
                            f, a, x_ = n // 3, (dnh, dnl, dnh)[n % 3], (ah, ah, al)[n % 3]
                            ins = pe.matmul(ps[:, 4 + j % 4, :], a[:, f, t * P:(t + 1) * P], x_[:, f, b * HALF:(b + 1) * HALF],
                                            start=n == 0, stop=n == 5)
                        ins.then_inc(down_done, 1)

                up(0, 0)
                pe.wait_ge(sq_added, l * 14 + 14)
                for b in range(2):
                    ins = pe.matmul(ps[:, 4 + b, :], ones, rstd[:, b * HALF:(b + 1) * HALF], start=True, stop=True)
                ins.then_inc(stat_done, 1)
                up(1, 1)
                with pe.Fori(1, GROUPS) as i:
                    up(i * 2, 0)
                    down(i - 1)
                    up(i * 2 + 1, 1)
                pe.wait_ge(u_ready, l * FT + FT)
                down(GROUPS - 1)
                meet(pe, l, 3)

            for b in range(2):
                ins = pe.matmul(ps[:, 4 + b, :], ones, rstd[:, b * HALF:(b + 1) * HALF], start=True, stop=True)
            ins.then_inc(stat_done, 1)
            for t in range(KT):
                pe.wait_ge(fin_ready, t + 1)
                if t >= 2:
                    pe.wait_ge(fin_copied, t - 1)
                for m in range(TT):
                    ins = pe.transpose(ps[:, 2 * (t % 2) + m // 4, (m % 4) * P:(m % 4 + 1) * P], z[:, t % 2, m * P:(m + 1) * P], ident)
                ins.then_inc(fin_trans, 1)


def shape_constants():
    f = np.float32
    cst = np.zeros((P, CW), f)
    cst[:, C_ID:C_ID + P] = np.eye(P)
    cst[:, C_ONE:C_ONE + P] = 1.0
    cst[:, C_BLK:C_BLK + P] = np.kron(np.eye(2), np.ones((HD, HD)))
    for t in range(2):
        for p in range(P):
            cst[p, C_SC + t] = SCALE_C / SLOPES[2 * t + p // HD]
    cst[:, C_SC + 2:C_SC + 4] = 1.0
    cst[:, C_EPS] = EPS
    j = np.arange(DW)[None, :] - (T - P)
    dist = np.abs(np.arange(P)[:, None] - j).astype(np.float16)

    def rope(dim, copies):
        nf = dim // 4
        inv = (f(10000.0) ** (-np.arange(nf, dtype=f) / f(nf))).astype(f)
        rows, cols = (np.arange(T) // GRID_W).astype(f), (np.arange(T) % GRID_W).astype(f)
        parts_c, parts_s = [], []
        for pos in (rows, cols):
            ang = (inv[:, None] * pos[None, :]).astype(f)
            c, s = np.cos(ang).astype(f), np.sin(ang).astype(f)
            parts_c += [c, c]
            parts_s += [-s, s]
        return np.stack([np.tile(np.concatenate(parts_c), (copies, 1)), np.tile(np.concatenate(parts_s), (copies, 1))]).astype(f)

    import math
    li = np.array([[0.8 - 0.6 * math.exp(-0.3 * i), 1.0 - (0.8 - 0.6 * math.exp(-0.3 * i))] for i in range(L)], f)
    return cst, dist, rope(HD, 2), rope(ROPE, 1), li


def kernel(**inputs):
    import concourse.bacc as bacc
    from concourse.bass_utils import run_bass_kernel_spmd

    f = np.float32
    a = {k: np.ascontiguousarray(v) for k, v in inputs.items()}
    cst, dist, rope_a, rope_b, li = shape_constants()

    def columns(v):
        return np.ascontiguousarray(v.reshape(-1, P).T)

    norms = list(a["norm_attn"]) + [a["final_norm"]]
    vecs = np.zeros((L, P, VW), f)
    for i in range(L):
        v = vecs[i]
        v[:, V_NEXT:V_NEXT + KT] = columns(norms[i + 1])
        v[:, V_FFN:V_FFN + KT] = columns(a["norm_ffn"][i])
        v[:, V_QG] = np.tile(a["q_norm_a"][i], 2)
        v[:, V_KG] = np.tile(a["k_norm_a"][i], 2)
        v[:, V_CQG] = a["q_a_norm_b"][i][:P]
        v[0:QR - P, V_CQG + 1] = a["q_a_norm_b"][i][P:]
        v[:, V_CKVG] = a["kv_a_norm_b"][i]
        v[:, V_SUB] = np.tile(a["subln_c"][i], 2)
        for n, name in enumerate(("lambda_q1_c", "lambda_k1_c", "lambda_q2_c", "lambda_k2_c")):
            v[:, V_LAM + n * CQK:V_LAM + (n + 1) * CQK] = a[name][i]
        for n in range(3):
            v[:, V_CONV + 2 * n * FT:V_CONV + 2 * (n + 1) * FT] = columns(a["conv_w"][i, n])
        v[:, V_CONV + 6 * FT:V_CONV + 8 * FT] = columns(a["conv_b"][i])
        v[:, V_LI:V_LI + 2] = li[i]
    arrays = dict(x=a["x"].reshape(T, D), first_gain=columns(norms[0]), w_in=a["w_in"], w_uq=a["w_uq_b"], w_ukv=a["w_ukv_b"],
                  w_out=a["w_out"], w_up=a["w_up"], w_down=a["w_down"], vecs=vecs, consts=cst, dist=dist, rope_a=rope_a, rope_b=rope_b)
    nc = bacc.Bacc("TRN2", target_bir_lowering=False, num_devices=1)
    aps = [nc.dram_tensor(f"in_{k}", v.shape, mybir.dt.from_np(v.dtype), kind="ExternalInput").ap() for k, v in arrays.items()]
    out = nc.dram_tensor("out_0", (T, D), F32, kind="ExternalOutput").ap()
    build(nc, *aps, out)
    res = run_bass_kernel_spmd(nc, [{f"in_{k}": v for k, v in arrays.items()}], core_ids=[0])
    return res.results[0]["out_0"].reshape(1, T, D)
```

```python
from contextlib import ExitStack

import numpy as np

import concourse.bass as bass
from concourse import mybir

F32 = mybir.dt.float32
F32R = mybir.dt.float32r
F16 = mybir.dt.float16
ALU = mybir.AluOpType
ACT = mybir.ActivationFunctionType
AX = mybir.AxisListType

P = 128
L, T, D = 2, 1024, 1024
KT = D // P
TT = T // P
HALF = 512
HD = 64
NA, NKV, NB, NC = 8, 2, 4, 4
QR, KVR, NOPE, ROPE = 192, 128, 64, 32
CQK = 32
FF = 2816
FT = FF // P
GROUPS = FT // 2
EPS = 1e-6
GRID_W = 64

A_Q, A_K, A_V = 0, 512, 640
B_CQ, B_CKV, B_KR = 768, 960, 1088
C_Q, C_K, C_V = 1120, 1376, 1632

TILES = [("cq0", B_CQ), ("cq1", B_CQ + P), ("ckv", B_CKV), ("kr", B_KR)]
TILES += [("aq", A_Q + P * i) for i in range(4)] + [("ak", A_K)]
TILES += [("cq_", C_Q), ("cq_", C_Q + P), ("ck_", C_K), ("ck_", C_K + P)]
TILES += [("v", A_V), ("v", C_V), ("v", C_V + P)]
NT = len(TILES)
ITEMS = [0, 1, 2, 3, "uq", "ukv"] + list(range(4, NT))
NI = len(ITEMS)
JOBS = {0: [("sx", 0)], 2: [("scq", 0)], 3: [("sckv", 0)], 4: [("uq", h) for h in range(4)],
        5: [("sa", 4), ("ukv", 0), ("ukv", 1), ("tr", 0), ("ukv", 2), ("tr", 1), ("ukv", 3), ("tr", 2), ("tr", 3)],
        6: [("sa", 5)], 7: [("sa", 6)], 8: [("sa", 7)], 9: [("sa", 8)],
        14: [("tv", 13)], 15: [("tv", 14), ("tv", 15)]}
JOB_LIST = [j for t in range(NT) for j in JOBS.get(t, [])]
NJ = len(JOB_LIST)
AHEAD = {3: 3}
SQUARED = [0, 1, 2, 4, 5, 6, 7, 8]

V_NEXT, V_FFN, V_QG, V_KG, V_CQG, V_CKVG, V_SUB, V_LAM = 0, 8, 16, 17, 18, 20, 21, 22
V_CONV = V_LAM + 4 * CQK
V_LI = V_CONV + 4 * 2 * FT
VW = V_LI + 2
C_ID, C_ONE, C_BLK, C_SC, C_EPS = 0, P, 2 * P, 3 * P, 3 * P + 4
CW = C_EPS + 2
DW = 2 * T - P

SLOPES = [2.0 ** (-8.0 * (h + 1) / NC) for h in range(NC)]
SCALE_B = (NOPE + ROPE) ** -0.5
SCALE_C = CQK ** -0.5

HEADS = [("A", h) for h in range(NA)] + [("B", h) for h in range(NB)] + [("C", h) for h in range(NC)]
NU = 2 * len(HEADS)
U_C = 2 * (NA + NB)


def items_before(u):
    return 4 * u + 4 * (u - U_C) if isinstance(u, int) and u > U_C else u * 4


NS = 4 * NU + 4 * (NU - U_C)
STEP_OF = {4: {0: [0], 1: [1], 3: [2], 5: [3]}, 8: {0: [0, 1], 1: [2], 2: [3], 3: [4], 4: [5], 5: [6, 7]}}
EXP_STEP_OF = {4: {1: [0], 2: [1], 4: [2], 6: [3]}, 8: {0: [0], 1: [1], 2: [2], 3: [3], 4: [4], 5: [5, 6], 6: [7]}}
HI_STEPS = {"A": (0, 3), "B": (0, 3), "C": (2, 4)}
MIX_STEPS = (2, 4, 6, 7)
USES = NA + NB + 2 * NC
STEPS = {"pool layer": 24, "pool units": 2, "dve layer": 246, "dve units": 0, "dve group": 6}
PT_CREDIT, EXP_CREDIT, AV_CREDIT, O_CREDIT, N_CREDIT, MIX_CREDIT = 2, 2, 4, 2, 1, 1
LAG = 2
NPT = 4


def build(nc, x_in, first_gain, w_in, w_uq, w_ukv, w_out, w_up, w_down, vecs, consts, dist, rope_a, rope_b, out):
    def dram(name, shape):
        return nc.dram_tensor(name, shape, F32).ap()

    qa_d, ka_d = dram("qa_d", (NA * HD, T)), dram("ka_d", (NKV * HD, T))
    qb_d, kb_d = dram("qb_d", (NB * 96, T)), dram("kb_d", (NB * 96, T))
    qc_d, kc_d = dram("qc_d", (NC * 2 * CQK, T)), dram("kc_d", (NC * 2 * CQK, T))
    v_d = dram("v_d", (T, (NKV + NC + NB) * HD))
    x_d = dram("x_d", (KT, P, T))

    ctx = ExitStack()
    with ctx:
        def sb(stack, name, shape, dt=F32):
            return stack.enter_context(nc.sbuf_tensor(name, shape, dt))

        xgh, xgl = sb(ctx, "xgh", [P, KT, T], F32R), sb(ctx, "xgl", [P, KT, T], F32R)
        vec, cst = sb(ctx, "vec", [P, VW]), sb(ctx, "cst", [P, CW])
        gain0 = sb(ctx, "gain0", [P, KT])
        small = sb(ctx, "small", [P, 8])
        wraw = sb(ctx, "wraw", [P, 2 * KT * P])
        w0h, w0l = sb(ctx, "w0h", [P, 2 * KT * P], F32R), sb(ctx, "w0l", [P, 2 * KT * P], F32R)
        ident, ones, blk = cst[:, C_ID:C_ID + P], cst[:, C_ONE:C_ONE + P], cst[:, C_BLK:C_BLK + P]
        eps = cst[:, C_EPS:C_EPS + 1]

        ph13 = ExitStack()
        xT, rstd = sb(ph13, "xT", [P, KT, T]), sb(ph13, "rstd", [P, T])

        ph1 = ExitStack()
        ra, rb_ = sb(ph1, "ra", [P, 2, T]), sb(ph1, "rb_", [P, 2, T])
        z, sq, r = sb(ph1, "z", [P, 2, T]), sb(ph1, "sq", [P, T]), sb(ph1, "r", [P, T])
        e = sb(ph1, "e", [P, 2, T])
        vt = sb(ph1, "vt", [P, TT, P])
        ch, cl = sb(ph1, "ch", [P, 3, T], F32R), sb(ph1, "cl", [P, 3, T], F32R)
        wqh, wql = sb(ph1, "wqh", [P, 2, 384], F32R), sb(ph1, "wql", [P, 2, 384], F32R)
        wkh, wkl = sb(ph1, "wkh", [P, 512], F32R), sb(ph1, "wkl", [P, 512], F32R)
        ph1.close()

        ph3 = ExitStack()
        w1h, w1l = sb(ph3, "w1h", [P, 2 * KT * P], F32R), sb(ph3, "w1l", [P, 2 * KT * P], F32R)
        draw = sb(ph3, "draw", [P, 2, D])
        dnh, dnl = sb(ph3, "dnh", [P, 2, D], F32R), sb(ph3, "dnl", [P, 2, D], F32R)
        ah, al = sb(ph3, "ah", [P, 2, T], F32R), sb(ph3, "al", [P, 2, T], F32R)
        u, cv = sb(ph3, "u", [P, 2, T + 2]), sb(ph3, "cv", [P, 2, T])
        sq3 = sb(ph3, "sq3", [P, T])
        ph3.close()
        ph13.close()

        ph2 = ExitStack()
        raw = sb(ph2, "raw", [P, 2, T])
        stack = [[sb(ph2, f"stack{p}{s}", [P, T], F32R) for s in range(4)] for p in range(2)]
        prob, prob1 = sb(ph2, "prob", [P, 2, 4, T]), sb(ph2, "prob1", [P, 2, T])
        pth, ptl = sb(ph2, "pth", [P, NPT, HALF], F32R), sb(ph2, "ptl", [P, NPT, HALF], F32R)
        vraw = sb(ph2, "vraw", [P, TT, HD])
        vst = [sb(ph2, f"vst{p}", [P, TT, P], F32R) for p in range(2)]
        dtab = sb(ph2, "dtab", [P, DW], F16)
        diag, nrm = sb(ph2, "diag", [P, 4, P]), sb(ph2, "nrm", [P, HALF])
        osum = sb(ph2, "osum", [P, HALF])
        mx, nmx = sb(ph2, "mx", [P, 2, 8]), sb(ph2, "nmx", [P, 2, 8])
        dinv = sb(ph2, "dinv", [P, 4])
        rsum, rinv = sb(ph2, "rsum", [P, 2, 8]), sb(ph2, "rinv", [P, 2, 8])
        ph2.close()

        ps = ctx.enter_context(nc.psum_tensor("ps", [P, 8, HALF], F32))

        def sem(name):
            return ctx.enter_context(nc.semaphore(name))

        fence = sem("fence")
        settled = {n: sem("settled_" + n) for n in ("PE", "DVE", "Activation", "Pool", "SP")}
        x_loaded, const_loaded, vec_loaded = sem("x_loaded"), sem("const_loaded"), sem("vec_loaded")
        dve_step, pool_step = sem("dve_step"), sem("pool_step")
        xt_done = sem("xt_done")
        x_final, x_squared, sq_added, xg_hi, xg_lo = (sem(n) for n in ("x_final", "x_squared", "sq_added", "xg_hi", "xg_lo"))
        wraw_full = [sem("wraw_full0"), sem("wraw_full1")]
        w_hi, w_lo, proj_done, z_ready = sem("w_hi"), sem("w_lo"), sem("proj_done"), sem("z_ready")
        sq_ready, sq_free, job_ready, job_free = sem("sq_ready"), sem("sq_free"), sem("job_ready"), sem("job_free")
        r_free, latent_ready, out_ready = sem("r_free"), sem("latent_ready"), sem("out_ready")
        roped, z_stored, e_stored = sem("roped"), [sem("z_stored0"), sem("z_stored1")], [sem("e_stored0"), sem("e_stored1")]
        vt_stored, x_stored, rope_loaded = sem("vt_stored"), sem("x_stored"), sem("rope_loaded")
        raw_full, raw_free = [sem("rawq_full"), sem("rawk_full")], [sem("rawq_free"), sem("rawk_free")]
        vraw_full, vraw_free = sem("vraw_full"), sem("vraw_free")
        dtab_loaded = sem("dtab_loaded")
        scores_done, max_done, exp_done, mixed = sem("scores_done"), sem("max_done"), sem("exp_done"), sem("mixed")
        trans_done, pt_hi, pt_lo, av_done = sem("trans_done"), sem("pt_hi"), sem("pt_lo"), sem("av_done")
        ratio_done, map_scaled, mixed_first, dinv_done, diag_done, norm_done, norm_copied, part_copied, o_read, o_ready, mix_hi, mix_lo = (
            sem(n) for n in ("ratio_done", "map_scaled", "mixed_first", "dinv_done", "diag_done", "norm_done", "norm_copied", "part_copied", "o_read", "o_ready", "mix_hi", "mix_lo"))
        raw_hi = [sem("rawq_hi"), sem("rawk_hi")]
        lam_exp = sem("lam_exp")
        up_full, up_hi, up_lo, dn_full, dn_hi, dn_lo = (sem(n) for n in ("up_full", "up_hi", "up_lo", "dn_full", "dn_hi", "dn_lo"))
        out_full = [sem("out_full0"), sem("out_full1")]
        x_back = [sem(f"x_back{t}") for t in range(KT)]
        c_summed, c_squared, c_stat, c_root, c_normed, c_hi, c_lo = (
            sem(n) for n in ("c_summed", "c_squared", "c_stat", "c_root", "c_normed", "c_hi", "c_lo"))
        op_done, stat_done, root_done, rstd_done = sem("op_done"), sem("stat_done"), sem("root_done"), sem("rstd_done")
        up_done, u_ready, tap_mid, conv_done, silu_done, prod_done, a_hi, a_lo = (
            sem(n) for n in ("up_done", "u_ready", "tap_mid", "conv_done", "silu_done", "prod_done", "a_hi", "a_lo"))
        down_done, y_done = sem("down_done"), sem("y_done")
        fin_ready, fin_trans, fin_copied, out_stored = sem("fin_ready"), sem("fin_trans"), sem("fin_copied"), [sem(f"out_stored{i}") for i in range(4)]

        def settle(eng):
            eng.sem_inc(settled[eng.engine.name], 1)

        def meet(eng, l, n):
            settle(eng)
            eng.drain().then_inc(fence, 1)
            eng.wait_ge(fence, l * 15 + 5 * n + 5)

        class Steps:

            def __init__(self, eng, s):
                self.eng, self.s, self.base, self.n = eng, s, 0, 0

            def __call__(self, ins):
                self.n += 1
                ins.then_inc(self.s, 1)
                self.eng.wait_ge(self.s, self.base + self.n)

            def enter(self, i, loop, first=0):
                was = (self.base, self.n)
                self.base, self.n = (i - first) * STEPS[loop] + (self.base + self.n), 0
                return was

            def leave(self, was, loop, passes):
                assert self.n == STEPS[loop], f"STEPS {loop} = {self.n}"
                self.base, self.n = was[0], was[1] + STEPS[loop] * passes

        def raw_dmas(n):
            return sum(2 if ITEMS[m] == "uq" else 1 for m in range(n % 2, n + 1, 2))

        RAWS = [raw_dmas(NI - 2 + (NI + p) % 2) for p in range(2)]
        Z_OUT = [t for t in range(NT) if TILES[t][0] in ("kr", "aq", "ak", "cq_", "ck_")]

        def z_dmas(t):
            return NB if TILES[t][0] == "kr" else 1

        def z_stores(t):
            return sum(z_dmas(m) for m in Z_OUT if m <= t and m % 2 == t % 2)

        ZS = [z_stores(14), z_stores(15)]

        def job_no(kind, a):
            return JOB_LIST.index((kind, a))

        READY = [x for x in JOB_LIST if x[0] not in ("scq", "sckv", "sa")]
        NR = len(READY)

        def ready_no(kind, a):
            return READY.index((kind, a))

        def item_no(t):
            return ITEMS.index(t)

        stage = [z[:, 0, :], z[:, 1, :], e[:, 0, :], e[:, 1, :], ra[:, 0, :], ra[:, 1, :], rb_[:, 0, :], rb_[:, 1, :]]

        def out_slot(t):
            return (e, ra)[t // 2 % 2][:, t % 2, :]

        def two(ap):
            return ap.rearrange("p (b n) -> p b n", b=2)

        STAGED = 2 * NA + NB + 4 * 2 * NC
        USE0 = {"A": 0, "B": NA, "C": NA + NB}
        HEAD0 = {"A": 0, "B": NA, "C": NA + NB}

        def wslot(w, i):
            return w[:, i * KT * P:(i + 1) * KT * P]

        def up_weights(par):
            return ((w1h, w1l), (w0h, w0l))[par]

        def head(hh):
            return ("A", hh) if hh < NA else ("B", hh - NA) if hh < NA + NB else ("C", hh - NA - NB)

        def unit(k, j=0):
            group = head(k // 2)[0]
            hh = j * 2 + k // 2
            return dict(group=group, par=k // 2 % 2, half=k % 2, u=j * 4 + k, hh=hh, h=hh - HEAD0[group], tile=j + k // 4,
                        k=k, items=8 if group == "C" else 4, item0=items_before(k) if isinstance(j, int) and j == 0 else j * 16 + 4 * k)

        def operands_ahead(x):
            for hh, i in ((x["k"] // 2 + 1, 0), (x["k"] // 2 + 1, 1), (x["k"] // 2 + 2, 0)):
                if hh < NA + NB + NC:
                    c = head(hh)[0] == "C"
                    at = 2 * hh - 3 if c and i == 0 else 2 * hh - 2
                    if x["k"] == at and (c or i == 0):
                        return head(hh)[0], hh, i, x["hh"] + (hh - x["k"] // 2)
            return None

        LOOP_K = 4
        LOOPS = 3

        def run_units(fn, eng, step=None, after_first=None, loop="dve units"):
            fn(unit(0), None, unit(1))
            if after_first:
                after_first()
            with eng.Fori(0, LOOPS) as j:
                was = step.enter(j, loop) if step else None
                for k in range(1, LOOP_K + 1):
                    fn(unit(k, j), unit(k - 1, j), unit(k + 1, j))
            if step:
                step.leave(was, loop, LOOPS)
            for k in range(LOOPS * LOOP_K + 1, NU):
                fn(unit(k), unit(k - 1), unit(k + 1) if k + 1 < NU else None)

        def part_rows(x):
            low, high = slice(0, HD), slice(HD, P)
            return (low, high) if x["par"] == 0 else (high, low)

        def mix_at(t_, x):
            p0, c0 = HD * x["par"], x["half"] * HALF
            return t_[p0:p0 + HD, bass.ds(x["tile"], 1), c0:c0 + HALF].rearrange("p a n -> p (a n)")

        block = ctx.enter_context(nc.Block())

        @block.sync
        def _(sp):
            sp.dma_start(cst[:, :], consts).then_inc(const_loaded, 16)
            sp.dma_start(gain0[:, :], first_gain).then_inc(const_loaded, 16)
            for m in range(TT):
                sp.dma_start(stage[m], x_in[m * P:(m + 1) * P, :]).then_inc(x_loaded, 16)
            def raw_load(l, n, wait=True, row=None):
                row = l if row is None else row
                if wait:
                    sp.wait_ge(w_lo, l * NI + n - 1)
                    settle(sp)
                it, w, full = ITEMS[n], wslot(wraw, n % 2), wraw_full[n % 2]
                if it == "uq":
                    sp.dma_start(w[:, 0:384], w_uq[bass.ds(row, 1), 0:P, :].rearrange("a p n -> p (a n)")).then_inc(full, 16)
                    sp.dma_start(w[0:QR - P, 384:768], w_uq[bass.ds(row, 1), P:QR, :].rearrange("a p n -> p (a n)")).then_inc(full, 16)
                elif it == "ukv":
                    sp.dma_start(w[:, 0:512], w_ukv[bass.ds(row, 1), :, :].rearrange("a p n -> p (a n)")).then_inc(full, 16)
                else:
                    c = TILES[it][1]
                    sp.dma_start(w.rearrange("p (k n) -> p k n", k=KT),
                                 w_in[bass.ds(row, 1), :, c:c + P].rearrange("a (k p) n -> p (a k) n", p=P)).then_inc(full, 16)

            for n in range(4):
                raw_load(0, n, wait=n >= 2)
            meet(sp, 0, 0)

            with sp.Fori(0, L) as l:
                sp.dma_start(vec[:, :], vecs[bass.ds(l, 1), :, :].rearrange("a p n -> p (a n)")).then_inc(vec_loaded, 16)
                for i in range(2):
                    sp.dma_start(ra[:, i, :], rope_a[i]).then_inc(rope_loaded, 16)
                    for p0 in (0, 64):
                        sp.dma_start(rb_[p0:p0 + ROPE, i, :], rope_b[i]).then_inc(rope_loaded, 16)
                sp.dma_start(x_d.rearrange("k p t -> p k t"), xT[:, :, :]).then_inc(x_stored, 16)

                def store_z(t):
                    if t <= 8:
                        sp.wait_ge(out_ready, l * 6 + t - 2)
                    else:
                        sp.wait_ge(z_ready, l * NT + t + 1)
                    kind = TILES[t][0]
                    if kind == "kr":
                        for h in range(NB):
                            sp.dma_start(kb_d[h * 96 + NOPE:(h + 1) * 96, :], z[0:ROPE, t % 2, :]).then_inc(z_stored[t % 2], 16)
                        return
                    dst = {"aq": qa_d, "ak": ka_d, "cq_": qc_d, "ck_": kc_d}[kind]
                    n = [m for m in range(NT) if TILES[m][0] == kind].index(t)
                    sp.dma_start(dst[n * P:(n + 1) * P, :], z[:, t % 2, :]).then_inc(z_stored[t % 2], 16)

                def store_job(kind, h):
                    if kind == "uq":
                        sp.wait_ge(roped, l * NB + h + 1)
                        sp.dma_start(qb_d[h * 96:(h + 1) * 96, :], e[0:96, h % 2, :]).then_inc(e_stored[h % 2], 16)
                        return
                    sp.wait_ge(job_free, l * NJ + job_no(kind, h) + 1)
                    v_rows = v_d.rearrange("(m p) c -> p m c", p=P)
                    if kind == "ukv":
                        sp.dma_start(kb_d[h * 96:h * 96 + NOPE, :], e[0:NOPE, h % 2, :]).then_inc(e_stored[h % 2], 16)
                    elif kind == "tr":
                        sp.dma_start(v_rows[:, :, (6 + h) * HD:(7 + h) * HD], vt[:, :, 0:HD]).then_inc(vt_stored, 16)
                    else:
                        src = e[:, 0, :].rearrange("p (m c) -> p m c", m=TT) if h == 15 else vt[:, :, :]
                        sp.dma_start(v_rows[:, :, (h - 13) * P:(h - 12) * P], src).then_inc(vt_stored, 16)

                n = 4
                for t in range(NT):
                    while n < NI and n <= item_no(t) + AHEAD.get(t, 2):
                        raw_load(l, n)
                        n += 1
                    if t == 4:
                        store_z(3)
                    if t == 5:
                        for h in range(NB):
                            store_job("uq", h)
                    if t == 6:
                        for kind, h in JOBS[5][1:]:
                            store_job(kind, h)
                    if 6 <= t <= 10:
                        store_z(t - 2)
                    if 11 <= t <= 14:
                        store_z(t - 2)
                def load_operands(group, h, v):
                    src_q, src_k, rows, copies = {"A": (qa_d, ka_d, HD, 2), "B": (qb_d, kb_d, 96, 1), "C": (qc_d, kc_d, CQK, 4)}[group]
                    maps = 2 if group == "C" else 1
                    for i in range(maps):
                        n_ = h * maps + i
                        for s, (src, row) in enumerate(((src_q, n_ * rows), (src_k, (v if group == "A" else n_) * rows))):
                            sp.wait_ge(raw_free[s], l * USES + USE0[group] + n_ + 1)
                            for c in range(copies):
                                sp.dma_start(raw[c * (P // copies):c * (P // copies) + rows, s, :], src[bass.ds(row, rows), :]).then_inc(raw_full[s], 16)

                def load_values(group, h, v):
                    sp.wait_ge(vraw_free, l * (NA + NB + NC) + HEAD0[group] + h + 1)
                    settle(sp)
                    col = {"A": v, "B": h + 6, "C": h + 2}[group] * HD
                    sp.dma_start(vraw[:, :, :], v_d.rearrange("(m p) c -> p m c", p=P)[:, :, bass.ds(col, HD)]).then_inc(vraw_full, 16)

                def load_head(group, h, v):
                    load_operands(group, h, v)
                    load_values(group, h, v)

                sp.wait_ge(z_stored[0], l * (16 * ZS[0]) + 16 * z_stores(8))
                settle(sp)
                sp.wait_ge(x_stored, l * 16 + 16)
                settle(sp)
                load_operands("A", 0, 0)
                for kind, h in JOBS[14] + JOBS[15]:
                    store_job(kind, h)
                for p in range(2):
                    sp.wait_ge(z_stored[p], l * (16 * ZS[p]) + 16 * ZS[p])
                    sp.wait_ge(e_stored[p], l * 64 + 64)
                settle(sp)
                sp.wait_ge(vt_stored, l * (7 * 16) + 7 * 16)
                meet(sp, l, 1)
                settle(sp)


                def load_out(t):
                    if t >= 2:
                        sp.wait_ge(up_lo, l * (KT + FT) + t - 1)
                    sp.dma_start(wslot(wraw, t % 2).rearrange("p (k n) -> p k n", k=KT),
                                 w_out[bass.ds(l, 1), :, t * P:(t + 1) * P].rearrange("a (k p) n -> p (a k) n", p=P)).then_inc(out_full[t % 2], 16)

                load_values("A", 0, 0)
                sp.dma_start(dtab[:, :], dist).then_inc(dtab_loaded, 16)
                load_out(0)
                load_out(1)
                with sp.Fori(1, NA // NKV) as hh:
                    load_head("A", hh, 0)
                with sp.Fori(NA // NKV, NA) as hh:
                    load_head("A", hh, 1)
                with sp.Fori(0, NB) as h:
                    load_head("B", h, h)
                with sp.Fori(0, NC) as h:
                    load_head("C", h, h)
                meet(sp, l, 2)

                def load_up(f):
                    sp.wait_ge(up_lo, l * (KT + FT) + KT + f)
                    v3 = wraw[:, :].rearrange("p (k c n) -> p k c n", k=KT, c=2)
                    for c in range(2):
                        sp.dma_start(v3[:, :, c, :], w_up[bass.ds(l, 1), :, bass.ds(f * P + c * FF, P)].rearrange("a (k p) n -> p (a k) n", p=P)).then_inc(up_full, 16)

                def load_down(g):
                    if not (isinstance(g, int) and g == 0):
                        sp.wait_ge(dn_lo, l * GROUPS + g)
                    sp.dma_start(draw[:, :, :], w_down[bass.ds(l, 1), bass.ds(g * (2 * P), 2 * P), :].rearrange("a (c p) n -> p (a c) n", p=P)).then_inc(dn_full, 16)

                for t in range(KT):
                    sp.dma_start(xT[:, t, :], x_d[t]).then_inc(x_back[t], 16)
                load_down(0)
                for t in range(2, KT):
                    load_out(t)
                for f in range(3):
                    load_up(f)
                with sp.Fori(1, GROUPS - 1) as i:
                    load_up(i * 2 + 1)
                    load_up(i * 2 + 2)
                    load_down(i)
                load_up(FT - 1)
                load_down(GROUPS - 1)
                sp.wait_ge(up_lo, (l + 1) * (KT + FT))
                settle(sp)
                for n in range(4):
                    raw_load(l + 1, n, wait=n >= 2, row=(l + 1) % L)
                meet(sp, l, 3)
                settle(sp)

            for t in range(KT):
                sp.wait_ge(fin_copied, t + 1)
                sp.dma_start(out.rearrange("(m p) d -> p m d", p=P)[:, :, t * P:(t + 1) * P],
                             out_slot(t).rearrange("p (m d) -> p m d", m=TT)).then_inc(out_stored[t % 4], 16)
            for s in out_stored:
                sp.wait_ge(s, 16 * KT // 4)

        @block.gpsimd
        def _(pool):
            step = Steps(pool, pool_step)
            for s in (raw_free[0], raw_free[1], vraw_free):
                pool.memset(small[0:1, 7:8], 0.0).then_inc(s, 1)
                pool.wait_ge(s, 1)

            def add_squares(n0, s0, sq_bufs):
                for t in range(1, KT):
                    pool.wait_ge(x_squared, n0 + t + 1)
                    if t > 1:
                        pool.wait_ge(sq_added, s0 + t - 1)
                    pool.tensor_tensor(rstd[:, :], rstd[:, :], sq_bufs[t % len(sq_bufs)], ALU.add).then_inc(sq_added, 1)

            def lo_item(l, n):
                it, w = ITEMS[n], wslot(wraw, n % 2)
                pool.wait_ge(w_hi, l * NI + n + 1)
                if it == "uq":
                    pool.tensor_tensor(wql[:, 0, :], w[:, 0:384], wqh[:, 0, :].bitcast(F32), ALU.subtract)
                    pool.tensor_tensor(wql[0:64, 1, :], w[0:64, 384:768], wqh[0:64, 1, :].bitcast(F32), ALU.subtract).then_inc(w_lo, 1)
                elif it == "ukv":
                    pool.tensor_tensor(wkl[:, :], w[:, 0:512], wkh[:, :].bitcast(F32), ALU.subtract).then_inc(w_lo, 1)
                else:
                    pool.tensor_tensor(wslot(w0l, it % 2), w, wslot(w0h, it % 2).bitcast(F32), ALU.subtract).then_inc(w_lo, 1)

            for n in range(2):
                lo_item(0, n)
            add_squares(0, 0, [sq[:, :]])
            meet(pool, 0, 0)

            with pool.Fori(0, L) as l:
                was = step.enter(l, "pool layer")
                for n in range(2, NI):
                    lo_item(l, n)
                def lo_operand(hh, i, s, h=None):
                    group, st = head(hh)[0], stack[hh % 2]
                    h = hh if h is None else h
                    n_ = h * 2 - (NA + NB) + i if group == "C" else h
                    src = raw[:, s, :]
                    pool.wait_ge(raw_hi[s], l * USES + n_ + 1)
                    if group == "B":
                        pool.tensor_tensor(st[2 * s + 1][0:96, :], src[0:96, :], st[2 * s][0:96, :].bitcast(F32), ALU.subtract).then_inc(raw_free[s], 1)
                    elif group == "A" and s:
                        pool.tensor_tensor(st[2][:, :], src, st[1][:, :].bitcast(F32), ALU.subtract).then_inc(raw_free[s], 1)
                    else:
                        dst = st[0] if group == "A" else st[2 * i + s]
                        for a, b in ([(64, 128)] if group == "A" or s else [(32, 64), (96, 128)]):
                            ins = pool.tensor_tensor(dst[a:b, :], src[a:b, :], dst[a:b, :].bitcast(F32), ALU.subtract)
                            if a == 32:
                                step(ins)
                        ins.then_inc(raw_free[s], 1)
                    pool.wait_ge(raw_free[s], l * USES + n_ + 2)

                pool.wait_ge(w_lo, l * NI + NI)
                for s in range(2):
                    lo_operand(0, 0, s)
                meet(pool, l, 1)

                def hi_values(hh, h=None):
                    h = hh if h is None else h
                    pool.wait_ge(vraw_full, (l * (NA + NB + NC) + h + 1) * 16)
                    settle(pool)
                    if hh:
                        pool.wait_ge(av_done, l * (8 * NU) + h * 16 - 16 + AV_CREDIT)
                        settle(pool)
                    step(pool.tensor_copy(vst[hh % 2][:, :, 0:HD], vraw[:, :, :]))

                def lo_values(hh, h=None):
                    h = hh if h is None else h
                    v = vst[hh % 2]
                    pool.tensor_tensor(v[:, :, HD:P], vraw[:, :, :], v[:, :, 0:HD].bitcast(F32), ALU.subtract).then_inc(vraw_free, 1)
                    pool.wait_ge(vraw_free, l * (NA + NB + NC) + h + 2)

                def diagonals(x):
                    pool.wait_ge(dinv_done, l * NU + x["u"] + 1)
                    if not (isinstance(x["u"], int) and x["u"] == 0):
                        pool.wait_ge(norm_done, l * NU + x["u"])
                    pool.tensor_tensor(diag[:, :, :], ident.unsqueeze(1).to_broadcast([P, 4, P]), dinv[:, :].unsqueeze(2).to_broadcast([P, 4, P]),
                                       ALU.mult).then_inc(diag_done, 1)
                    pool.wait_ge(diag_done, l * NU + x["u"] + 1)

                def scale_output(x):
                    rows = slice(HD * x["par"], HD * x["par"] + HD)
                    pool.wait_ge(o_read, l * NU + x["u"] + 1 + O_CREDIT)
                    pool.wait_ge(norm_copied, l * NU + x["u"] + 1 + N_CREDIT)
                    pool.tensor_tensor(osum[rows, :], osum[rows, :], nrm[rows, :], ALU.mult).then_inc(o_ready, 1)
                    pool.wait_ge(o_ready, l * NU + x["u"] + 1 + O_CREDIT)

                def lo_mix(x):
                    rows = slice(HD * x["par"], HD * x["par"] + HD)
                    pool.wait_ge(mix_hi, l * NU + x["u"] + 1)
                    pool.tensor_tensor(mix_at(xgl, x), osum[rows, :], mix_at(xgh, x).bitcast(F32), ALU.subtract).then_inc(mix_lo, 1)
                    pool.wait_ge(mix_lo, l * NU + x["u"] + 1 + MIX_CREDIT)

                def mix_first(x):
                    b, n = x["half"], l * (2 * NC) + x["u"] - U_C + 1
                    pool.wait_ge(map_scaled, n)
                    pool.tensor_tensor(prob[:, b, 0, :], prob1[:, 0, :], prob[:, b, 0, :], ALU.add).then_inc(mixed_first, 1)
                    pool.wait_ge(mixed_first, n)

                def pool_unit(x, prev, nx):
                    hh, h = x["k"] // 2 + 1, x["hh"] + 1
                    more = hh < NA + NB + NC
                    ahead = operands_ahead(x)
                    late = ahead and ahead[0] == "C"
                    diagonals(x)
                    if ahead and not late:
                        lo_operand(ahead[1], ahead[2], 0, ahead[3])
                    if nx and nx["group"] == "C":
                        mix_first(nx)
                    if ahead:
                        lo_operand(ahead[1], ahead[2], 0 if late else 1, ahead[3])
                    if prev:
                        scale_output(prev)
                    if x["half"] == 1 and more:
                        hi_values(hh, h)
                    if late:
                        lo_operand(ahead[1], ahead[2], 1, ahead[3])
                    if x["half"] == 1 and more:
                        lo_values(hh, h)
                    if prev:
                        lo_mix(prev)

                def lo_out(t):
                    pool.wait_ge(up_hi, l * (KT + FT) + t + 1)
                    pool.tensor_tensor(wslot(w0l, t % 2), wslot(wraw, t % 2), wslot(w0h, t % 2).bitcast(F32), ALU.subtract).then_inc(up_lo, 1)

                hi_values(0)
                lo_values(0)

                def first_out():
                    lo_out(0)
                    lo_out(1)
                    pool.wait_ge(up_lo, l * (KT + FT) + 2)
                    settle(pool)

                run_units(pool_unit, pool, step, first_out, "pool units")
                scale_output(unit(NU - 1))
                lo_mix(unit(NU - 1))
                meet(pool, l, 2)

                def lo_up(f, par):
                    pool.wait_ge(up_hi, l * (KT + FT) + KT + f + 1)
                    pool.tensor_tensor(up_weights(par)[1][:, :], wraw[:, :], up_weights(par)[0][:, :].bitcast(F32), ALU.subtract).then_inc(up_lo, 1)

                def lo_down(g):
                    pool.wait_ge(dn_hi, l * GROUPS + g + 1)
                    pool.tensor_tensor(dnl[:, :, :], draw[:, :, :], dnh[:, :, :].bitcast(F32), ALU.subtract).then_inc(dn_lo, 1)

                def add_square(t):
                    pool.wait_ge(x_squared, l * 16 + 8 + t + 1)
                    if t > 1:
                        pool.wait_ge(sq_added, l * 14 + 7 + t - 1)
                    pool.tensor_tensor(rstd[:, :], rstd[:, :], sq3[:, :], ALU.add).then_inc(sq_added, 1)

                for t in range(2, KT):
                    lo_out(t)
                    if t >= 3:
                        add_square(t - 2)
                add_square(6)
                lo_up(0, 0)
                add_square(7)
                lo_up(1, 1)
                lo_down(0)
                lo_up(2, 0)
                with pool.Fori(1, GROUPS - 1) as i:
                    lo_up(i * 2 + 1, 1)
                    lo_up(i * 2 + 2, 0)
                    lo_down(i)
                lo_up(FT - 1, 1)
                lo_down(GROUPS - 1)
                for n in range(2):
                    lo_item(l + 1, n)
                add_squares(l * 16 + 16, l * 14 + 14, [cv[:, 0, :], cv[:, 1, :]])
                meet(pool, l, 3)
            step.leave(was, "pool layer", L)

        @block.scalar
        def _(act):
            def gained(t, gain, final):
                act.wait_ge(*final)
                act.activation(xgh[:, t, :], xT[:, t, :], ACT.Identity, scale=gain[:, t:t + 1]).then_inc(xg_hi, 1)

            def square(t, final, s0, *bufs):
                act.wait_ge(*final)
                if t > len(bufs):
                    act.wait_ge(sq_added, s0 + t - len(bufs))
                act.activation(rstd[:, :] if t == 0 else bufs[t % len(bufs)], xT[:, t, :], ACT.Square).then_inc(x_squared, 1)

            def hi_item(l, n, wait=True):
                it, w = ITEMS[n], wslot(wraw, n % 2)
                act.wait_ge(wraw_full[n % 2], (l * RAWS[n % 2] + raw_dmas(n)) * 16)
                if it == "uq":
                    act.activation(wqh[:, 0, :], w[:, 0:384], ACT.Copy)
                    act.activation(wqh[0:64, 1, :], w[0:64, 384:768], ACT.Copy).then_inc(w_hi, 1)
                elif it == "ukv":
                    act.activation(wkh[:, :], w[:, 0:512], ACT.Copy).then_inc(w_hi, 1)
                else:
                    if wait:
                        act.wait_ge(proj_done, l * NT + it - 1)
                    act.activation(wslot(w0h, it % 2), w, ACT.Copy).then_inc(w_hi, 1)

            for n in range(2):
                hi_item(0, n, wait=False)
            act.wait_ge(const_loaded, 32)
            for t in range(KT):
                gained(t, gain0, (x_final, t + 1))
                square(t, (x_final, t + 1), 0, sq[:, :])
            meet(act, 0, 0)

            with act.Fori(0, L) as l:
                def root(j, dst, scale, bias=eps):
                    act.activation(two(dst), ps[:, 4 + 2 * (j % 2):6 + 2 * (j % 2), :], ACT.Sqrt, bias=bias, scale=scale).then_inc(job_free, 1)

                def job(kind, a):
                    j = job_no(kind, a)
                    if kind in ("scq", "sckv", "sa"):
                        act.wait_ge(sq_free, l * len(SQUARED) + {"scq": 2, "sckv": 3}.get(kind, a))
                    else:
                        act.wait_ge(job_ready, l * NR + ready_no(kind, a) + 1)
                    src = ps[:, 4 + 2 * (j % 2):6 + 2 * (j % 2), :]
                    if kind in ("sx", "scq", "sckv", "sa"):
                        if kind == "scq":
                            act.wait_ge(r_free, l + 1)
                        elif kind == "sckv":
                            act.wait_ge(latent_ready, l * 2 + 1)
                        elif kind == "sa" and a == 4:
                            act.wait_ge(roped, l * NB + NB)
                        elif kind == "sa":
                            act.wait_ge(out_ready, l * 6 + a - 3)
                        if kind == "sa" and a < 8:
                            root(j, r[:, :], 1.0, cst[:, C_EPS + 1:C_EPS + 2])
                            return
                        root(j, r[:, :], {"sx": 1.0 / D, "scq": 1.0 / QR, "sckv": 1.0 / KVR, "sa": 1.0 / HD}[kind])
                    elif kind == "uq":
                        if a >= 2:
                            act.wait_ge(e_stored[a % 2], l * 64 + 16)
                        act.activation(two(e[0:96, a % 2, :]), src[0:96], ACT.Copy, scale=SCALE_B).then_inc(job_free, 1)
                    elif kind == "ukv":
                        act.wait_ge(e_stored[a % 2], l * 64 + 16 * (2 + a // 2))
                        if a >= 2:
                            act.wait_ge(job_ready, l * NR + ready_no("tr", a - 2) + 1)
                        act.activation(two(e[:, a % 2, :]), src, ACT.Copy).then_inc(job_free, 1)
                    else:
                        n = [x for x in JOB_LIST if x[0] in ("tr", "tv")].index((kind, a))
                        if n == 6:
                            act.wait_ge(e_stored[0], l * 64 + 64)
                        elif n:
                            act.wait_ge(vt_stored, l * (7 * 16) + 16 * n)
                        s4 = src.rearrange("p b (m c) -> p (b m) c", m=4)
                        if kind == "tr":
                            act.activation(vt[:, :, 0:HD], s4[:, :, HD:P], ACT.Copy).then_inc(job_free, 1)
                        elif n == 6:
                            act.activation(e[:, 0, :].rearrange("p (m c) -> p m c", m=TT), s4, ACT.Copy).then_inc(job_free, 1)
                        else:
                            act.activation(vt[:, :, :], s4, ACT.Copy).then_inc(job_free, 1)

                def hi_operand(hh, i, s, h=None):
                    group, st = head(hh)[0], stack[hh % 2]
                    h = hh if h is None else h
                    n_ = h * 2 - (NA + NB) + i if group == "C" else h
                    dmas = {"A": n_ * 2 + 2, "B": n_ + NA + 1, "C": n_ * 4 + (2 * NA + NB - 4 * (NA + NB) + 4)}[group]
                    act.wait_ge(raw_full[s], (l * STAGED + dmas) * 16)
                    rows = 96 if group == "B" else P
                    dst = st[{"A": s, "B": 2 * s, "C": 2 * i + s}[group]]
                    act.activation(dst[0:rows, :], raw[0:rows, s, :], ACT.Copy).then_inc(raw_hi[s], 1)

                nxt = 2
                for t in range(NT):
                    while nxt < NI and nxt <= item_no(t) + AHEAD.get(t, 2):
                        hi_item(l, nxt)
                        nxt += 1
                    for kind, a in JOBS.get(t, []):
                        job(kind, a)
                    if t == 14:
                        for q in range(2):
                            hi_operand(0, 0, q)
                    if t in SQUARED:
                        act.wait_ge(z_ready, l * NT + t + 1)
                        n = SQUARED.index(t)
                        if n:
                            act.wait_ge(sq_free, l * len(SQUARED) + n)
                        act.activation(sq[:, :], z[:, t % 2, :], ACT.Square).then_inc(sq_ready, 1)
                meet(act, l, 1)

                act.activation(small[:, 2:4], small[:, 0:2], ACT.Exp).then_inc(lam_exp, 1)

                def exp_item(x, i):
                    it, b = x["item0"] + i, x["half"]
                    act.wait_ge(max_done, l * NS + it + 1)
                    if x["group"] == "C":
                        dst = prob1[:, i // 2 % 2, :] if i % 2 else prob[:, b, i // 2, :]
                        if i % 2:
                            n = 3 * (x["u"] - U_C) + i // 2 - 2
                            if i == 5:
                                act.wait_ge(mixed_first, l * (2 * NC) + x["u"] - U_C + 1)
                            elif n > 0:
                                act.wait_ge(mixed, l * (6 * NC) + n)
                        scale = SLOPES[x["h"]]
                    else:
                        dst, scale = prob[:, b, i, :], 1.0
                    act.activation(two(dst), ps[:, 2 * (i % 2):2 * (i % 2) + 2, :], ACT.Exp, bias=nmx[:, b, i:i + 1],
                                   scale=scale, accum_out=rsum[:, b, i:i + 1]).then_inc(exp_done, 1)

                def copy_norm(x):
                    act.wait_ge(norm_done, l * NU + x["u"] + 1)
                    act.wait_ge(o_ready, l * NU + x["u"] + O_CREDIT)
                    act.activation(nrm[:, :], ps[:, 7 - x["half"], :], ACT.Copy).then_inc(norm_copied, 1)

                def copy_part(x):
                    here, there = part_rows(x)
                    act.wait_ge(mix_lo, l * NU + x["u"] + MIX_CREDIT)
                    act.wait_ge(av_done, l * (8 * NU) + x["u"] * 8 + 8 + AV_CREDIT)
                    act.activation(osum[there, :], ps[here, 6 + x["half"], :], ACT.Copy).then_inc(part_copied, 1)

                def hi_mix(x):
                    act.wait_ge(o_ready, l * NU + x["u"] + 1 + O_CREDIT)
                    rows = slice(HD * x["par"], HD * x["par"] + HD)
                    act.activation(mix_at(xgh, x), osum[rows, :], ACT.Copy).then_inc(mix_hi, 1)

                def scale_map(x):
                    act.wait_ge(ratio_done, l * (2 * NC) + x["u"] - U_C + 1)
                    act.activation(prob1[:, 0, :], prob1[:, 0, :], ACT.Copy, scale=rinv[:, x["half"], 1:2]).then_inc(map_scaled, 1)

                def act_unit(x, prev, nx):
                    for s in range(8):
                        act.wait_ge(trans_done, l * (8 * NU) + x["u"] * 8 + s + 1)
                        act.wait_ge(av_done, l * (8 * NU) + x["u"] * 8 + s + 1 - NPT + AV_CREDIT)
                        act.activation(pth[:, s % NPT, :], ps[:, 4 + s % 2, :], ACT.Copy).then_inc(pt_hi, 1)
                        for i in EXP_STEP_OF[nx["items"]].get(s, ()) if nx else ():
                            exp_item(nx, i)
                        if s == 2 and prev:
                            copy_part(prev)
                        if s == 3 and nx and nx["group"] == "C":
                            scale_map(nx)
                        if s == 6 and prev:
                            hi_mix(prev)
                        if s == 6:
                            copy_norm(x)
                        ahead = operands_ahead(x)
                        if ahead and s in HI_STEPS[ahead[0]]:
                            hi_operand(ahead[1], ahead[2], HI_STEPS[ahead[0]].index(s), ahead[3])

                def hi_out(t):
                    act.wait_ge(out_full[t % 2], (l * (KT // 2) + t // 2 + 1) * 16)
                    if t >= 2:
                        act.wait_ge(op_done, l * KT + t - 1)
                    act.activation(wslot(w0h, t % 2), wslot(wraw, t % 2), ACT.Copy).then_inc(up_hi, 1)

                for i in range(4):
                    exp_item(unit(0), i)
                run_units(act_unit, act, after_first=lambda: (hi_out(0), hi_out(1)))
                last = unit(NU - 1)
                copy_part(last)
                hi_mix(last)
                meet(act, l, 2)

                def hi_up(f, par):
                    act.wait_ge(up_full, (l * (2 * FT) + f * 2 + 2) * 16)
                    if not isinstance(f, int) or f >= 2:
                        act.wait_ge(up_done, l * FT + f - 1)
                    elif f == 1:
                        act.wait_ge(op_done, l * KT + KT)
                    act.activation(up_weights(par)[0][:, :], wraw[:, :], ACT.Copy).then_inc(up_hi, 1)

                def hi_down(g):
                    act.wait_ge(dn_full, (l * GROUPS + g + 1) * 16)
                    if not (isinstance(g, int) and g == 0):
                        act.wait_ge(down_done, l * (16 * GROUPS) + g * 16)
                    act.activation(dnh[:, :, :], draw[:, :, :], ACT.Copy).then_inc(dn_hi, 1)

                for c in range(2):
                    act.wait_ge(c_summed, l * 2 + c + 1)
                    act.activation(cv[:, c, :], u[:, c, 0:T], ACT.Square).then_inc(c_squared, 1)
                for c in range(2):
                    act.wait_ge(c_stat, l * 2 + c + 1)
                    act.activation(two(cv[:, c, :]), ps[:, 4 + 2 * c:6 + 2 * c, :], ACT.Sqrt, bias=eps, scale=1.0 / HD).then_inc(c_root, 1)
                for c in range(2):
                    act.wait_ge(c_normed, l * 2 + c + 1)
                    act.activation(xgh[:, 6 + c, :], cv[:, c, :], ACT.Copy).then_inc(c_hi, 1)
                for t in range(2, KT):
                    hi_out(t)
                    square(t - 2, (x_final, l * KT + KT + t - 2 + 1), l * 14 + 7, sq3[:, :])
                hi_up(0, 0)
                square(6, (x_final, l * KT + KT + 6 + 1), l * 14 + 7, sq3[:, :])
                act.wait_ge(vec_loaded, l * 16 + 16)
                act.wait_ge(op_done, l * KT + KT)
                for t in range(KT):
                    gained(t, vec[:, V_FFN:V_FFN + KT], (x_final, l * KT + KT + t + 1))
                square(7, (x_final, l * KT + KT + 7 + 1), l * 14 + 7, sq3[:, :])
                hi_up(1, 1)
                act.wait_ge(stat_done, l + 1)
                act.activation(two(sq3[:, :]), ps[:, 4:6, :], ACT.Sqrt, bias=eps, scale=1.0 / D).then_inc(root_done, 1)
                hi_down(0)

                def mid_taps(f):
                    act.wait_ge(u_ready, l * FT + f + 1)
                    if not (isinstance(f, int) and f == 0):
                        act.wait_ge(a_lo, l * FT + f)
                    for c in range(2):
                        ins = act.activation(cv[:, c, :], u[:, c, 1:T + 1], ACT.Identity,
                                             scale=vec[:, bass.ds(f + (V_CONV + 2 * FT + c * FT), 1)],
                                             bias=vec[:, bass.ds(f + (V_CONV + 6 * FT + c * FT), 1)])
                    ins.then_inc(tap_mid, 1)

                def gate(f):
                    act.wait_ge(conv_done, l * FT + f + 1)
                    act.activation(cv[:, 0, :], cv[:, 0, :], ACT.Silu).then_inc(silu_done, 1)

                def hi_a(f, par):
                    act.wait_ge(prod_done, l * FT + f + 1)
                    if not (isinstance(f, int) and f < 2):
                        act.wait_ge(down_done, l * (16 * GROUPS) + (f - par) * 8)
                    act.activation(ah[:, par, :], cv[:, 0, :], ACT.Copy).then_inc(a_hi, 1)

                mid_taps(0)
                hi_up(2, 0)
                gate(0)
                hi_a(0, 0)
                mid_taps(1)
                gate(1)
                hi_a(1, 1)

                def act_group(i, last):
                    mid_taps(i * 2)
                    hi_up(i * 2 + 1, 1)
                    gate(i * 2)
                    if not last:
                        hi_up(i * 2 + 2, 0)
                    hi_a(i * 2, 0)
                    hi_down(i)
                    mid_taps(i * 2 + 1)
                    gate(i * 2 + 1)
                    hi_a(i * 2 + 1, 1)

                with act.Fori(1, GROUPS - 1) as i:
                    act_group(i, False)
                act_group(GROUPS - 1, True)
                act.wait_ge(up_done, l * FT + FT)
                for n in range(2):
                    hi_item(l + 1, n, wait=False)
                for t in range(KT):
                    final = (y_done, (l + 1) * (16 * GROUPS) - 16 + 2 * t + 2)
                    gained(t, vec[:, V_NEXT:V_NEXT + KT], final)
                    square(t, final, l * 14 + 14, cv[:, 0, :], cv[:, 1, :])
                meet(act, l, 3)

            act.wait_ge(stat_done, L + 1)
            act.activation(r[:, 0:TT], ps[:, 4, 0:TT], ACT.Sqrt, bias=eps, scale=1.0 / D).then_inc(root_done, 1)
            for t in range(KT):
                if t >= 2:
                    act.wait_ge(fin_trans, t - 1)
                act.activation(z[:, t % 2, :], xT[:, t, :], ACT.Identity, scale=vec[:, V_NEXT + t:V_NEXT + t + 1]).then_inc(fin_ready, 1)

        @block.vector
        def _(dve):
            step = Steps(dve, dve_step)
            for s, n in ((pt_lo, PT_CREDIT), (exp_done, EXP_CREDIT), (av_done, AV_CREDIT), (o_read, O_CREDIT), (o_ready, O_CREDIT), (norm_copied, N_CREDIT), (mix_lo, MIX_CREDIT)):
                for c in range(n):
                    dve.memset(small[64:65, 6:7], 0.0).then_inc(s, 1)
                    dve.wait_ge(s, c + 1)

            def lo_gained(t, n, gain):
                dve.wait_ge(xg_hi, n)
                dve.scalar_tensor_tensor(xgl[:, t, :], xT[:, t, :], gain[:, t:t + 1], xgh[:, t, :].bitcast(F32),
                                         ALU.mult, ALU.subtract).then_inc(xg_lo, 1)

            dve.wait_ge(const_loaded, 32)
            for t in range(KT):
                dve.wait_ge(xt_done, t + 1)
                dve.tensor_copy(two(xT[:, t, :]), ps[:, 2 * (t % 2):2 * (t % 2) + 2, :]).then_inc(x_final, 1)
                if t:
                    lo_gained(t - 1, t, gain0)
            lo_gained(KT - 1, KT, gain0)
            meet(dve, 0, 0)

            with dve.Fori(0, L) as l:
                was = step.enter(l, "dve layer")

                def evacuate(t):
                    dve.wait_ge(proj_done, l * NT + t + 1)
                    zz = z[:, t % 2, :]
                    if t >= 2 and t - 2 in Z_OUT:
                        dve.wait_ge(z_stored[t % 2], (l * ZS[t % 2] + z_stores(t - 2)) * 16)
                    if t == 15:
                        dve.wait_ge(job_ready, l * NR + ready_no("tv", 13) + 1)
                    for b in range(2):
                        src, dst, rs = ps[:, 2 * (t % 2) + b, :], zz[:, b * HALF:(b + 1) * HALF], rstd[:, b * HALF:(b + 1) * HALF]
                        if t in (9, 10, 11, 12):
                            ins = dve.scalar_tensor_tensor(dst, src, cst[:, C_SC + t - 9:C_SC + t - 8], rs, ALU.mult, ALU.mult)
                        else:
                            ins = dve.tensor_tensor(dst, src, rs, ALU.mult)
                    ins.then_inc(z_ready, 1)
                    dve.wait_ge(z_ready, l * NT + t + 1)

                def rope(v, tab, r0, r1, shift):
                    mask = [j // (2 * shift) * 2 * shift + (j + shift) % (2 * shift) for j in range(32)]
                    settle(dve)
                    step(dve.stream_shuffle(r[r0:r1, :], v[r0:r1, :], mask))
                    step(dve.tensor_tensor(r[r0:r1, :], r[r0:r1, :], tab[r0:r1, 1, :], ALU.mult))
                    step(dve.tensor_tensor(v[r0:r1, :], v[r0:r1, :], tab[r0:r1, 0, :], ALU.mult))
                    return dve.tensor_tensor(v[r0:r1, :], v[r0:r1, :], r[r0:r1, :], ALU.add)

                def latent(t, slot, gain, rows):
                    zz = z[0:rows, t % 2, :]
                    step(dve.scalar_tensor_tensor(zz, zz, gain, r[0:rows, :], ALU.mult, ALU.mult))
                    step(dve.tensor_copy(ch[0:rows, slot, :], zz))
                    return dve.tensor_tensor(cl[0:rows, slot, :], zz, ch[0:rows, slot, :].bitcast(F32), ALU.subtract)

                def wait_root(kind, a=0):
                    dve.wait_ge(job_free, l * NJ + job_no(kind, a) + 1)

                def per_head(t):
                    wait_root("sa", t)
                    zz = z[:, t % 2, :]
                    g = V_QG if t < 8 else V_KG
                    step(dve.reciprocal(r[:, :], r[:, :]))
                    step(dve.scalar_tensor_tensor(zz, zz, vec[:, g:g + 1], r[:, :], ALU.mult, ALU.mult))
                    rope(zz, ra, 0, P, 16).then_inc(out_ready, 1)
                    dve.wait_ge(out_ready, l * 6 + t - 2)

                wait_root("sx")
                dve.reciprocal(rstd[:, :], r[:, :]).then_inc(r_free, 1)
                dve.wait_ge(r_free, l + 1)
                evacuate(0)
                evacuate(1)
                dve.wait_ge(vec_loaded, l * 16 + 16)
                for i in range(2):
                    a, b = V_LAM + 2 * i * CQK, V_LAM + (2 * i + 1) * CQK
                    step(dve.tensor_tensor(vec[:, a:a + CQK], vec[:, a:a + CQK], vec[:, b:b + CQK], ALU.mult))
                    step(dve.tensor_reduce(small[:, i:i + 1], vec[:, a:a + CQK], AX.X, ALU.add))
                step(dve.tensor_tensor(small[:, 5:6], vec[:, V_SUB:V_SUB + 1], vec[:, V_LI + 1:V_LI + 2], ALU.mult))
                wait_root("scq")
                step(dve.reciprocal(r[:, :], r[:, :]))
                step(latent(0, 0, vec[:, V_CQG:V_CQG + 1], P))
                evacuate(2)
                latent(1, 1, vec[0:64, V_CQG + 1:V_CQG + 2], 64).then_inc(latent_ready, 1)
                dve.wait_ge(latent_ready, l * 2 + 1)
                evacuate(3)
                wait_root("sckv")
                step(dve.reciprocal(r[:, :], r[:, :]))
                latent(2, 2, vec[:, V_CKVG:V_CKVG + 1], P).then_inc(latent_ready, 1)
                dve.wait_ge(latent_ready, l * 2 + 2)
                dve.wait_ge(rope_loaded, (l + 1) * 6 * 16)
                rope(z[:, 1, :], rb_, 0, ROPE, 8).then_inc(out_ready, 1)
                dve.wait_ge(out_ready, l * 6 + 1)
                evacuate(4)
                for h in range(NB):
                    dve.wait_ge(job_free, l * NJ + job_no("uq", h) + 1)
                    rope(e[:, h % 2, :], rb_, NOPE, 96, 8).then_inc(roped, 1)
                    dve.wait_ge(roped, l * NB + h + 1)
                for t in range(5, NT):
                    evacuate(t)
                    if 4 <= t - 1 <= 8:
                        per_head(t - 1)
                meet(dve, l, 1)

                dve.wait_ge(lam_exp, l + 1)
                step(dve.tensor_tensor(small[:, 4:5], small[:, 3:4], small[:, 2:3], ALU.subtract))
                step(dve.tensor_tensor(small[:, 4:5], small[:, 4:5], vec[:, V_LI:V_LI + 1], ALU.subtract))
                dve.wait_ge(dtab_loaded, l * 16 + 16)

                def max_item(x, i):
                    b = x["half"]
                    dve.wait_ge(scores_done, l * NS + x["item0"] + i + 1)
                    src = ps[:, 2 * (i % 2):2 * (i % 2) + 2, :]
                    if x["group"] == "C":
                        off = T - P - P * (4 * b + i // 2)
                        scale = SLOPES[x["h"]]
                        settle(dve)
                        step(dve.tensor_tensor_reduce(src, src, two(dtab[:, off:off + T]), 1.0, -3.0e38, ALU.subtract, ALU.max, mx[:, b, i:i + 1]))
                    else:
                        dve.tensor_reduce(nmx[:, b, i:i + 1], src, AX.XY, ALU.max, negate=True).then_inc(max_done, 1)
                        return
                    dve.tensor_scalar(nmx[:, b, i:i + 1], mx[:, b, i:i + 1], -scale, None, ALU.mult).then_inc(max_done, 1)

                def mix_maps(x, i):
                    b = x["half"]
                    dve.wait_ge(exp_done, l * NS + x["item0"] + 2 * i + 2 + EXP_CREDIT)
                    a, c = slice(2 * i, 2 * i + 1), slice(2 * i + 1, 2 * i + 2)
                    step(dve.reciprocal(rinv[:, b, c], rsum[:, b, c]))
                    if i == 0:
                        dve.scalar_tensor_tensor(rinv[:, b, c], rsum[:, b, a], small[:, 4:5], rinv[:, b, c], ALU.mult, ALU.mult).then_inc(ratio_done, 1)
                        return
                    step(dve.scalar_tensor_tensor(rinv[:, b, c], rsum[:, b, a], small[:, 4:5], rinv[:, b, c], ALU.mult, ALU.mult))
                    dve.scalar_tensor_tensor(prob[:, b, i, :], prob1[:, i % 2, :], rinv[:, b, c], prob[:, b, i, :],
                                             ALU.mult, ALU.add).then_inc(mixed, 1)

                def reciprocal_sums(x):
                    b = x["half"]
                    sums = rsum[:, b, 0:8:2] if x["group"] == "C" else rsum[:, b, 0:4]
                    dve.wait_ge(exp_done, l * NS + x["item0"] + x["items"] + EXP_CREDIT)
                    if not (isinstance(x["u"], int) and x["u"] == 0):
                        dve.wait_ge(diag_done, l * NU + x["u"])
                    dve.reciprocal(dinv[:, 0:4], sums).then_inc(dinv_done, 1)

                def sum_output(x):
                    rows, there = slice(HD * x["par"], HD * x["par"] + HD), part_rows(x)[1]
                    dve.wait_ge(part_copied, l * NU + x["u"] + 1)
                    dve.tensor_tensor(osum[rows, :], ps[there, 6 + x["half"], :], osum[there, :], ALU.add).then_inc(o_read, 1)

                def dve_unit(x, prev, nx):
                    for s in range(8):
                        for i in STEP_OF[nx["items"]].get(s, ()) if nx else ():
                            max_item(nx, i)
                        if nx and nx["group"] == "C" and s in MIX_STEPS:
                            mix_maps(nx, MIX_STEPS.index(s))
                        dve.wait_ge(pt_hi, l * (8 * NU) + x["u"] * 8 + s + 1)
                        dve.tensor_tensor(ptl[:, s % NPT, :], ps[:, 4 + s % 2, :], pth[:, s % NPT, :].bitcast(F32), ALU.subtract).then_inc(pt_lo, 1)
                        if s == 0:
                            reciprocal_sums(x)
                        if s == 3 and prev:
                            sum_output(prev)

                for i in range(4):
                    max_item(unit(0), i)
                run_units(dve_unit, dve, step)
                sum_output(unit(NU - 1))
                meet(dve, l, 2)

                for c in range(2):
                    dve.tensor_tensor(u[:, c, 0:T], xgh[:, 6 + c, :].bitcast(F32), xgl[:, 6 + c, :].bitcast(F32), ALU.add).then_inc(c_summed, 1)
                for c in range(2):
                    dve.wait_ge(c_root, l * 2 + c + 1)
                    step(dve.reciprocal(cv[:, c, :], cv[:, c, :]))
                    dve.scalar_tensor_tensor(cv[:, c, :], u[:, c, 0:T], small[:, 5:6], cv[:, c, :], ALU.mult, ALU.mult).then_inc(c_normed, 1)
                for c in range(2):
                    dve.wait_ge(c_hi, l * 2 + c + 1)
                    dve.tensor_tensor(xgl[:, 6 + c, :], cv[:, c, :], xgh[:, 6 + c, :].bitcast(F32), ALU.subtract).then_inc(c_lo, 1)
                step(dve.memset(u[:, :, 0:1], 0.0))
                step(dve.memset(u[:, :, T + 1:T + 2], 0.0))
                for t in range(KT):
                    dve.wait_ge(op_done, l * KT + t + 1)
                    dve.wait_ge(x_back[t], l * 16 + 16)
                    dve.tensor_tensor(two(xT[:, t, :]), ps[:, 2 * (t % 2):2 * (t % 2) + 2, :], two(xT[:, t, :]), ALU.add).then_inc(x_final, 1)
                for t in range(KT):
                    lo_gained(t, l * 16 + 8 + t + 1, vec[:, V_FFN:V_FFN + KT])
                dve.wait_ge(root_done, l + 1)
                dve.reciprocal(rstd[:, :], sq3[:, :]).then_inc(rstd_done, 1)
                dve.wait_ge(rstd_done, l + 1)

                def conv_in(f, par):
                    dve.wait_ge(up_done, l * FT + f + 1)
                    for c in range(2):
                        for b in range(2):
                            ins = dve.tensor_tensor(u[:, c, 1 + b * HALF:1 + (b + 1) * HALF], ps[:, 4 * par + 2 * c + b, :],
                                                    rstd[:, b * HALF:(b + 1) * HALF], ALU.mult)
                    ins.then_inc(u_ready, 1)
                    dve.wait_ge(u_ready, l * FT + f + 1)

                def tap(f, c, k):
                    return dve.scalar_tensor_tensor(cv[:, c, :], u[:, c, k:k + T], vec[:, bass.ds(f + (V_CONV + 2 * k * FT + c * FT), 1)],
                                                    cv[:, c, :], ALU.mult, ALU.add)

                def outer_taps(f, c):
                    if c == 0:
                        dve.wait_ge(tap_mid, l * FT + f + 1)
                    step(tap(f, c, 0))
                    if c == 0:
                        tap(f, c, 2).then_inc(conv_done, 1)
                    else:
                        step(tap(f, c, 2))

                def gate_value(f):
                    dve.wait_ge(silu_done, l * FT + f + 1)
                    dve.tensor_tensor(cv[:, 0, :], cv[:, 0, :], cv[:, 1, :], ALU.mult).then_inc(prod_done, 1)

                def lo_a(f, par):
                    dve.wait_ge(a_hi, l * FT + f + 1)
                    dve.tensor_tensor(al[:, par, :], cv[:, 0, :], ah[:, par, :].bitcast(F32), ALU.subtract).then_inc(a_lo, 1)

                def add_down(g, j):
                    t, b = j // 2, j % 2
                    dve.wait_ge(down_done, l * (16 * GROUPS) + g * 16 + j + 1)
                    xs = xT[:, t, b * HALF:(b + 1) * HALF]
                    ins = dve.tensor_tensor(xs, ps[:, 4 + j % 4, :], xs, ALU.add)
                    ins.then_inc(y_done, 1)

                for f in range(2):
                    conv_in(f, f)
                    outer_taps(f, 0)
                    outer_taps(f, 1)
                    gate_value(f)
                    lo_a(f, f)

                def dve_group(i):
                    g = i - 1
                    conv_in(i * 2, 0)
                    for j in range(16):
                        add_down(g, j)
                        if j == 3:
                            outer_taps(i * 2, 0)
                        if j == 6:
                            outer_taps(i * 2, 1)
                        if j == 9:
                            gate_value(i * 2)
                    lo_a(i * 2, 0)
                    conv_in(i * 2 + 1, 1)
                    outer_taps(i * 2 + 1, 0)
                    outer_taps(i * 2 + 1, 1)
                    gate_value(i * 2 + 1)
                    lo_a(i * 2 + 1, 1)

                with dve.Fori(1, GROUPS) as i:
                    w2 = step.enter(i, "dve group", 1)
                    dve_group(i)
                step.leave(w2, "dve group", GROUPS - 1)
                for j in range(16):
                    add_down(GROUPS - 1, j)
                    if j % 2:
                        dve.wait_ge(y_done, l * (16 * GROUPS) + 16 * (GROUPS - 1) + j + 1)
                        if j > 2:
                            lo_gained(j // 2 - 1, l * 16 + 16 + j // 2, vec[:, V_NEXT:V_NEXT + KT])
                lo_gained(KT - 1, l * 16 + 24, vec[:, V_NEXT:V_NEXT + KT])
                meet(dve, l, 3)
            step.leave(was, "dve layer", L)

            dve.wait_ge(root_done, L + 1)
            dve.reciprocal(r[:, TT:2 * TT], r[:, 0:TT]).then_inc(rstd_done, 1)
            dve.wait_ge(rstd_done, L + 1)
            for t in range(KT):
                dve.wait_ge(fin_trans, t + 1)
                if t >= 4:
                    dve.wait_ge(out_stored[t % 4], 16 * (t // 4))
                dve.tensor_tensor(out_slot(t).rearrange("p (m d) -> p m d", m=TT),
                                  ps[:, 2 * (t % 2):2 * (t % 2) + 2, :].rearrange("p b (m d) -> p (b m) d", m=4),
                                  r[:, TT:2 * TT].unsqueeze(2).to_broadcast([P, TT, P]), ALU.mult).then_inc(fin_copied, 1)

        @block.tensor
        def _(pe):
            pe.wait_ge(const_loaded, 32)
            for t in range(KT):
                if t == 0:
                    pe.wait_ge(x_loaded, 16 * TT)
                if t >= 2:
                    pe.wait_ge(x_final, t - 1)
                for m in range(TT):
                    ins = pe.transpose(ps[:, 2 * (t % 2) + m // 4, (m % 4) * P:(m % 4 + 1) * P], stage[m][:, t * P:(t + 1) * P], ident)
                ins.then_inc(xt_done, 1)
            pe.drain().then_inc(fence, 1)

            def three(outs, wh_, wl_, xh, xl, start, stop):
                for n, (a, x_) in enumerate(((wh_, xh), (wl_, xh), (wh_, xl))):
                    for b in range(2):
                        ins = pe.matmul(outs[b], a, x_[:, b * HALF:(b + 1) * HALF], start=start and n == 0, stop=stop and n == 2)
                return ins

            with pe.Fori(0, L) as l:
                def project(t):
                    pe.wait_ge(w_lo, l * NI + item_no(t) + 1)
                    if t >= 2:
                        pe.wait_ge(z_ready, l * NT + t - 1)
                    if t == 0:
                        pe.wait_ge(x_final, l * KT + KT)
                    outs = [ps[:, 2 * (t % 2) + b, :] for b in range(2)]
                    for k in range(KT):
                        if t == 0:
                            pe.wait_ge(xg_lo, l * 16 + k + 1)
                        ins = three(outs, wslot(w0h, t % 2)[:, k * P:(k + 1) * P], wslot(w0l, t % 2)[:, k * P:(k + 1) * P],
                                    xgh[:, k, :], xgl[:, k, :], k == 0, k == KT - 1)
                    ins.then_inc(proj_done, 1)

                def bank(j, b):
                    return ps[:, 4 + 2 * (j % 2) + b, :]

                def squares_sum(j, n, lhsT, src, start, stop):
                    pe.wait_ge(sq_ready, l * len(SQUARED) + n + 1)
                    for b in range(2):
                        ins = pe.matmul(bank(j, b), lhsT, src[:, b * HALF:(b + 1) * HALF], start=start, stop=stop)
                    return ins

                def job(kind, a):
                    j = job_no(kind, a)
                    if j >= 2:
                        pe.wait_ge(job_free, l * NJ + j - 1)
                    if kind == "sx":
                        pe.wait_ge(sq_added, l * 14 + 7)
                        for b in range(2):
                            ins = pe.matmul(bank(j, b), ones, rstd[:, b * HALF:(b + 1) * HALF], start=True, stop=True)
                    elif kind == "scq":
                        squares_sum(j, 1, ones[0:64, :], sq[0:64, :], False, True).then_inc(sq_free, 1)
                        ins = None
                    elif kind in ("sckv", "sa"):
                        n = 2 if kind == "sckv" else a - 1
                        squares_sum(j, n, ones if kind == "sckv" else blk, sq[:, :], True, True).then_inc(sq_free, 1)
                        ins = None
                    elif kind == "uq":
                        if a == 0:
                            pe.wait_ge(w_lo, l * NI + item_no("uq") + 1)
                            pe.wait_ge(latent_ready, l * 2 + 1)
                        outs = [ps[0:96, 4 + 2 * (j % 2) + b, :] for b in range(2)]
                        for k, rows in ((0, P), (1, QR - P)):
                            ins = three(outs, wqh[0:rows, k, a * 96:(a + 1) * 96], wql[0:rows, k, a * 96:(a + 1) * 96],
                                        ch[0:rows, k, :], cl[0:rows, k, :], k == 0, k == 1)
                    elif kind == "ukv":
                        if a == 0:
                            pe.wait_ge(w_lo, l * NI + item_no("ukv") + 1)
                            pe.wait_ge(latent_ready, l * 2 + 2)
                        ins = three([bank(j, 0), bank(j, 1)], wkh[:, a * P:(a + 1) * P], wkl[:, a * P:(a + 1) * P],
                                    ch[:, 2, :], cl[:, 2, :], True, True)
                    else:
                        if kind == "tr":
                            pe.wait_ge(job_free, l * NJ + job_no("ukv", a) + 1)
                            src = e[:, a % 2, :]
                        else:
                            pe.wait_ge(z_ready, l * NT + a + 1)
                            src = z[:, a % 2, :]
                        for m in range(TT):
                            ins = pe.transpose(ps[:, 4 + 2 * (j % 2) + m // 4, (m % 4) * P:(m % 4 + 1) * P], src[:, m * P:(m + 1) * P], ident)
                    if ins is not None:
                        ins.then_inc(job_ready, 1)

                for t in range(NT):
                    project(t)
                    if t == 0:
                        pe.wait_ge(fence, l * 15 + 5)
                    if t == 1:
                        squares_sum(job_no("scq", 0), 0, ones, sq[:, :], True, False).then_inc(sq_free, 1)
                    for kind, a in JOBS.get(t, []):
                        job(kind, a)
                meet(pe, l, 1)

                def score_item(x, i):
                    it, st, b = x["item0"] + i, stack[x["par"]], x["half"]
                    if i == 0 and x["half"] == 0:
                        use = {"A": x["h"] + 1, "B": x["h"] + NA + 1, "C": x["h"] * 2 + (NA + NB + 2)}[x["group"]]
                        for q in range(2):
                            pe.wait_ge(raw_free[q], l * USES + use + 1)
                    pe.wait_ge(exp_done, l * NS + it - 1 + EXP_CREDIT)
                    qt = i // 2 if x["group"] == "C" else i
                    c0 = b * HALF + qt * P
                    if x["group"] == "A":
                        rows, terms = P, ((0, 1), (0, 2))
                    elif x["group"] == "B":
                        rows, terms = 96, ((0, 2), (1, 2), (0, 3))
                    else:
                        rows, terms = P, ((2 * (i % 2), 2 * (i % 2) + 1),)
                    for n, (q, k) in enumerate(terms):
                        for kh in range(2):
                            ins = pe.matmul(ps[:, 2 * (i % 2) + kh, :], st[q][0:rows, c0:c0 + P], st[k][0:rows, kh * HALF:(kh + 1) * HALF],
                                            start=n == 0, stop=n == len(terms) - 1)
                    ins.then_inc(scores_done, 1)

                def value_product(x, s):
                    b, v = x["half"], vst[x["par"]]
                    if s == 0:
                        pe.wait_ge(norm_copied, l * NU + x["u"] + N_CREDIT)
                        if x["half"] == 0:
                            pe.wait_ge(vraw_free, l * (NA + NB + NC) + x["hh"] + 2)
                    pe.wait_ge(pt_lo, l * (8 * NU) + x["u"] * 8 + s + 1 + PT_CREDIT)
                    pe.matmul(ps[:, 6 + b, :], v[:, s, :], pth[:, s % NPT, :], start=s == 0, stop=False)
                    pe.matmul(ps[:, 6 + b, :], v[:, s, :], ptl[:, s % NPT, :], start=False, stop=s == 7).then_inc(av_done, 1)

                def pe_unit(x, prev, nx):
                    b = x["half"]
                    for s in range(8):
                        items = STEP_OF[nx["items"]].get(s, ()) if nx else ()
                        early = s == 0 or nx and nx["group"] != "C"
                        if early:
                            for i in items:
                                score_item(nx, i)
                        if s == 0:
                            if x["group"] == "C":
                                pe.wait_ge(mixed_first, l * (2 * NC) + x["u"] - U_C + 1)
                                pe.wait_ge(mixed, l * (6 * NC) + 3 * (x["u"] - U_C) + 3)
                            else:
                                pe.wait_ge(exp_done, l * NS + x["item0"] + 4 + EXP_CREDIT)
                        pe.wait_ge(pt_lo, l * (8 * NU) + x["u"] * 8 + s - 1 + PT_CREDIT)
                        for m in range(4):
                            ins = pe.transpose(ps[:, 4 + s % 2, m * P:(m + 1) * P], prob[:, b, m, s * P:(s + 1) * P], ident)
                        ins.then_inc(trans_done, 1)
                        if not early:
                            for i in items:
                                score_item(nx, i)
                        if s >= LAG:
                            value_product(x, s - LAG)
                        elif prev:
                            value_product(prev, 8 + s - LAG)
                        if s == 5:
                            pe.wait_ge(diag_done, l * NU + x["u"] + 1)
                            pe.wait_ge(o_read, l * NU + x["u"] + O_CREDIT)
                            pe.matmul(ps[:, 7 - b, :], ones, diag[:, :, :].rearrange("p m n -> p (m n)"), start=True, stop=True).then_inc(norm_done, 1)

                for i in range(4):
                    score_item(unit(0), i)
                run_units(pe_unit, pe)
                for s in range(8 - LAG, 8):
                    value_product(unit(NU - 1), s)
                meet(pe, l, 2)

                def out_terms(t, k0, k1):
                    outs = [ps[:, 2 * (t % 2) + b, :] for b in range(2)]
                    for k in range(k0, k1):
                        ins = three(outs, wslot(w0h, t % 2)[:, k * P:(k + 1) * P], wslot(w0l, t % 2)[:, k * P:(k + 1) * P],
                                    xgh[:, k, :], xgl[:, k, :], k == 0, k == KT - 1)
                    return ins

                for t in range(2):
                    pe.wait_ge(up_lo, l * (KT + FT) + t + 1)
                    out_terms(t, 0, 3)
                    if t == 0:
                        for c in range(2):
                            pe.wait_ge(c_squared, l * 2 + c + 1)
                            for b in range(2):
                                ins = pe.matmul(ps[:, 4 + 2 * c + b, :], blk, cv[:, c, b * HALF:(b + 1) * HALF], start=True, stop=True)
                            ins.then_inc(c_stat, 1)
                    out_terms(t, 3, 6)
                for t in range(2):
                    for c in range(2):
                        if t == 0:
                            pe.wait_ge(c_lo, l * 2 + c + 1)
                        ins = out_terms(t, 6 + c, 7 + c)
                    ins.then_inc(op_done, 1)
                for t in range(2, KT):
                    pe.wait_ge(up_lo, l * (KT + FT) + t + 1)
                    pe.wait_ge(x_final, l * KT + KT + t - 1)
                    out_terms(t, 0, KT).then_inc(op_done, 1)

                def up(f, par):
                    pe.wait_ge(up_lo, l * (KT + FT) + KT + f + 1)
                    first = isinstance(f, int)
                    if first and f == 0:
                        pe.wait_ge(x_final, l * KT + KT + KT)
                    elif first and f == 1:
                        pe.wait_ge(root_done, l + 1)
                    elif par == 0:
                        pe.wait_ge(u_ready, l * FT + f - 1)
                    else:
                        pe.wait_ge(y_done, l * (16 * GROUPS) + f * 8 - 8)
                    for k in range(KT):
                        if first and f == 0:
                            pe.wait_ge(xg_lo, l * 16 + 8 + k + 1)
                        for c in range(2):
                            o = (2 * k + c) * P
                            outs = [ps[:, 4 * par + 2 * c + b, :] for b in range(2)]
                            ins = three(outs, up_weights(par)[0][:, o:o + P], up_weights(par)[1][:, o:o + P], xgh[:, k, :], xgl[:, k, :], k == 0, k == KT - 1)
                    ins.then_inc(up_done, 1)

                def down(g):
                    pe.wait_ge(dn_lo, l * GROUPS + g + 1)
                    pe.wait_ge(a_lo, l * FT + g * 2 + 2)
                    for j in range(16):
                        t, b = j // 2, j % 2
                        if j >= 4:
                            pe.wait_ge(y_done, l * (16 * GROUPS) + g * 16 + j - 3)
                        for n in range(6):
                            f, a, x_ = n // 3, (dnh, dnl, dnh)[n % 3], (ah, ah, al)[n % 3]
                            ins = pe.matmul(ps[:, 4 + j % 4, :], a[:, f, t * P:(t + 1) * P], x_[:, f, b * HALF:(b + 1) * HALF],
                                            start=n == 0, stop=n == 5)
                        ins.then_inc(down_done, 1)

                up(0, 0)
                pe.wait_ge(sq_added, l * 14 + 14)
                for b in range(2):
                    ins = pe.matmul(ps[:, 4 + b, :], ones, rstd[:, b * HALF:(b + 1) * HALF], start=True, stop=True)
                ins.then_inc(stat_done, 1)
                up(1, 1)
                with pe.Fori(1, GROUPS) as i:
                    up(i * 2, 0)
                    down(i - 1)
                    up(i * 2 + 1, 1)
                pe.wait_ge(u_ready, l * FT + FT)
                down(GROUPS - 1)
                pe.drain().then_inc(fence, 1)
            pe.wait_ge(fence, L * 15 + 5)

            for m in range(TT):
                ins = pe.matmul(ps[:, 4, m:m + 1], rstd[:, m * P:(m + 1) * P], ones[:, 0:1], start=True, stop=True)
            ins.then_inc(stat_done, 1)
            for t in range(KT):
                pe.wait_ge(fin_ready, t + 1)
                if t >= 2:
                    pe.wait_ge(fin_copied, t - 1)
                for m in range(TT):
                    ins = pe.transpose(ps[:, 2 * (t % 2) + m // 4, (m % 4) * P:(m % 4 + 1) * P], z[:, t % 2, m * P:(m + 1) * P], ident)
                ins.then_inc(fin_trans, 1)


def shape_constants():
    f = np.float32
    cst = np.zeros((P, CW), f)
    cst[:, C_ID:C_ID + P] = np.eye(P)
    cst[:, C_ONE:C_ONE + P] = 1.0
    cst[:, C_BLK:C_BLK + P] = np.kron(np.eye(2), np.ones((HD, HD)))
    for t in range(2):
        for p in range(P):
            cst[p, C_SC + t] = SCALE_C / SLOPES[2 * t + p // HD]
    cst[:, C_SC + 2:C_SC + 4] = 1.0
    cst[:, C_EPS], cst[:, C_EPS + 1] = EPS, EPS * HD
    j = np.arange(DW)[None, :] - (T - P)
    dist = np.abs(np.arange(P)[:, None] - j).astype(np.float16)

    def rope(dim, copies):
        nf = dim // 4
        inv = (f(10000.0) ** (-np.arange(nf, dtype=f) / f(nf))).astype(f)
        rows, cols = (np.arange(T) // GRID_W).astype(f), (np.arange(T) % GRID_W).astype(f)
        parts_c, parts_s = [], []
        for pos in (rows, cols):
            ang = (inv[:, None] * pos[None, :]).astype(f)
            c, s = np.cos(ang).astype(f), np.sin(ang).astype(f)
            parts_c += [c, c]
            parts_s += [-s, s]
        return np.stack([np.tile(np.concatenate(parts_c), (copies, 1)), np.tile(np.concatenate(parts_s), (copies, 1))]).astype(f)

    import math
    li = np.array([[0.8 - 0.6 * math.exp(-0.3 * i), 1.0 - (0.8 - 0.6 * math.exp(-0.3 * i))] for i in range(L)], f)
    return cst, dist, rope(HD, 2), rope(ROPE, 1), li


def kernel(**inputs):
    import concourse.bacc as bacc
    from concourse.bass_utils import run_bass_kernel_spmd

    f = np.float32
    a = {k: np.ascontiguousarray(v) for k, v in inputs.items()}
    cst, dist, rope_a, rope_b, li = shape_constants()

    def columns(v):
        return np.ascontiguousarray(v.reshape(-1, P).T)

    norms = list(a["norm_attn"]) + [a["final_norm"]]
    vecs = np.zeros((L, P, VW), f)
    for i in range(L):
        v = vecs[i]
        v[:, V_NEXT:V_NEXT + KT] = columns(norms[i + 1])
        v[:, V_FFN:V_FFN + KT] = columns(a["norm_ffn"][i])
        v[:, V_QG] = np.tile(a["q_norm_a"][i], 2)
        v[:, V_KG] = np.tile(a["k_norm_a"][i], 2)
        v[:, V_CQG] = a["q_a_norm_b"][i][:P]
        v[0:QR - P, V_CQG + 1] = a["q_a_norm_b"][i][P:]
        v[:, V_CKVG] = a["kv_a_norm_b"][i]
        v[:, V_SUB] = np.tile(a["subln_c"][i], 2)
        for n, name in enumerate(("lambda_q1_c", "lambda_k1_c", "lambda_q2_c", "lambda_k2_c")):
            v[:, V_LAM + n * CQK:V_LAM + (n + 1) * CQK] = a[name][i]
        for n in range(3):
            v[:, V_CONV + 2 * n * FT:V_CONV + 2 * (n + 1) * FT] = columns(a["conv_w"][i, n])
        v[:, V_CONV + 6 * FT:V_CONV + 8 * FT] = columns(a["conv_b"][i])
        v[:, V_LI:V_LI + 2] = li[i]
    arrays = dict(x=a["x"].reshape(T, D), first_gain=columns(norms[0]), w_in=a["w_in"], w_uq=a["w_uq_b"], w_ukv=a["w_ukv_b"],
                  w_out=a["w_out"], w_up=a["w_up"], w_down=a["w_down"], vecs=vecs, consts=cst, dist=dist, rope_a=rope_a, rope_b=rope_b)
    nc = bacc.Bacc("TRN2", target_bir_lowering=False, num_devices=1)
    aps = [nc.dram_tensor(f"in_{k}", v.shape, mybir.dt.from_np(v.dtype), kind="ExternalInput").ap() for k, v in arrays.items()]
    out = nc.dram_tensor("out_0", (T, D), F32, kind="ExternalOutput").ap()
    build(nc, *aps, out)
    res = run_bass_kernel_spmd(nc, [{f"in_{k}": v for k, v in arrays.items()}], core_ids=[0])
    return res.results[0]["out_0"].reshape(1, T, D)
```
